# Optimizing a Trainium2 kernel written in Bass

```python
import jax, jax.numpy as jnp
from jax import lax
import numpy as np

D_MODEL = 1024
BATCH = 1
SEQ = 1024
DEPTH = 2

A_HEADS = 8
A_HEAD_DIM = 64
A_WIDTH = A_HEADS * A_HEAD_DIM
DILATED_PATTERNS = ((128, 1), (512, 4), (2048, 16))
A_HALF_STEPS = 64
A_BLOCK = 64
REL_BUCKETS = 32
REL_MAX_DISTANCE = 1024
B_HEADS = 4
B_KEY_DIM = 128
B_VAL_DIM = 256
B_K_WIDTH = B_HEADS * B_KEY_DIM
B_V_WIDTH = B_HEADS * B_VAL_DIM
B_GATE_RANK = 16
B_GATE_NORMALIZER = 16.0
C_HEADS = 12
C_HEAD_DIM = 128
C_WIDTH = C_HEADS * C_HEAD_DIM
MIX_WIDTH = A_WIDTH + B_V_WIDTH
AB_IN_WIDTH = 3 * A_WIDTH + 2 * B_K_WIDTH + B_V_WIDTH + 2 * B_GATE_RANK + MIX_WIDTH
C_IN_WIDTH = 5 * C_WIDTH
CHUNK = 32
N_EVEN = (DEPTH + 1) // 2
N_ODD = DEPTH // 2
NORM_EPS = 1e-5
DEEPNORM_ALPHA = (2 * DEPTH) ** 0.25
DEEPNORM_BETA = (8 * DEPTH) ** -0.25


def _split(t, sizes):
    out, start = [], 0
    for n in sizes:
        out.append(t[..., start:start + n])
        start += n
    return out

def _t5_bucket(rel):
    half = REL_BUCKETS // 2
    max_exact = half // 2
    n = np.abs(rel)
    large = max_exact + (np.log(np.maximum(n, 1) / max_exact)
                         / np.log(REL_MAX_DISTANCE / max_exact) * (half - max_exact)).astype(np.int32)
    large = np.minimum(large, half - 1)
    return np.where(rel > 0, half, 0) + np.where(n < max_exact, n, large)

def _dilated_band_attention(q, k, v, rel_bias, dilation):
    Bsz, S, H, E = q.shape
    L = S // dilation
    nb = -(-L // A_BLOCK)
    Lp = nb * A_BLOCK

    def to_sub(t):
        return t.reshape(Bsz, L, dilation, H, E).transpose(0, 2, 1, 3, 4)

    qs, ks, vs = to_sub(q), to_sub(k), to_sub(v)
    qs = jnp.pad(qs, ((0, 0), (0, 0), (0, Lp - L), (0, 0), (0, 0))).reshape(Bsz, dilation, nb, A_BLOCK, H, E)

    def band(t):
        t = jnp.pad(t, ((0, 0), (0, 0), (A_BLOCK, Lp - L + A_BLOCK), (0, 0), (0, 0)))
        t = t.reshape(Bsz, dilation, nb + 2, A_BLOCK, H, E)
        return jnp.concatenate([t[:, :, :-2], t[:, :, 1:-1], t[:, :, 2:]], axis=3)

    kb, vb = band(ks), band(vs)
    qi = np.arange(A_BLOCK)[:, None]
    kj = np.arange(3 * A_BLOCK)[None, :]
    off = kj - A_BLOCK - qi
    key_idx = np.arange(nb)[:, None, None] * A_BLOCK + kj[None] - A_BLOCK
    mask = (np.abs(off) <= A_HALF_STEPS)[None] & (key_idx >= 0) & (key_idx < L)
    bias = jnp.transpose(rel_bias.astype(jnp.float32)[_t5_bucket(off * dilation)], (2, 0, 1))
    s = jnp.einsum('brnqhe,brnkhe->brnhqk', qs, kb) * (E ** -0.5) + bias
    s = jnp.where(mask[None, None, :, None], s, -jnp.inf)
    lse = jax.nn.logsumexp(s, axis=-1)
    p = jnp.exp(s - lse[..., None])
    o = jnp.einsum('brnhqk,brnkhe->brnqhe', p, vb).reshape(Bsz, dilation, Lp, H, E)[:, :, :L]
    o = o.transpose(0, 2, 1, 3, 4).reshape(Bsz, S, H, E)
    lse = lse.transpose(0, 1, 2, 4, 3).reshape(Bsz, dilation, Lp, H)[:, :, :L]
    lse = lse.transpose(0, 2, 1, 3).reshape(Bsz, S, H)
    return o, lse

def dilated_attention(q, k, v, rel_bias):
    outs, lses = [], []
    for _, dilation in DILATED_PATTERNS:
        o, lse = _dilated_band_attention(q, k, v, rel_bias, dilation)
        outs.append(o)
        lses.append(lse)
    w = jax.nn.softmax(jnp.stack(lses, 0), axis=0)
    return jnp.einsum('pbsh,pbshe->bshe', w, jnp.stack(outs, 0))

def _chunk_gated_scan(q, k, v, log_g):
    Bsz, S, H, K = q.shape
    V = v.shape[-1]
    N = S // CHUNK
    c = lambda t: t.reshape(Bsz, N, CHUNK, H, t.shape[-1])
    q, k, v, log_g = c(q), c(k), c(v), c(log_g)
    b = jnp.cumsum(log_g, axis=2)
    ref = b[:, :, CHUNK // 2 - 1:CHUNK // 2]
    s = jnp.einsum('bnthk,bnshk->bnhts', q * jnp.exp(b - ref), k * jnp.exp(ref - b))
    s = jnp.where(np.tril(np.ones((CHUNK, CHUNK), bool)), s, 0.0)
    o_intra = jnp.einsum('bnhts,bnshv->bnthv', s, v)
    b_last = b[:, :, -1]
    q_dec = q * jnp.exp(b)
    k_dec = k * jnp.exp(b_last[:, :, None] - b)

    def step(state, xs):
        qd, kd, vc, bl = xs
        o = jnp.einsum('bthk,bhkv->bthv', qd, state)
        state = jnp.exp(bl)[..., None] * state + jnp.einsum('bthk,bthv->bhkv', kd, vc)
        return state, o

    xs = (jnp.moveaxis(q_dec, 1, 0), jnp.moveaxis(k_dec, 1, 0), jnp.moveaxis(v, 1, 0), jnp.moveaxis(b_last, 1, 0))
    _, o_inter = lax.scan(step, jnp.zeros((Bsz, H, K, V), jnp.float32), xs)
    return (o_intra + jnp.moveaxis(o_inter, 0, 1)).reshape(Bsz, S, H, V)

def bidirectional_gated_scan(q, k_fwd, g_fwd, k_bwd, g_bwd, v):
    fwd = _chunk_gated_scan(q, k_fwd, v, g_fwd)
    flip = lambda t: jnp.flip(t, axis=1)
    bwd = flip(_chunk_gated_scan(flip(q), flip(k_bwd), flip(v), flip(g_bwd)))
    diag = jnp.sum(q * k_bwd, axis=-1, keepdims=True) * v
    return fwd + bwd - diag

def _head_rmsnorm(o, gain):
    o = o * lax.rsqrt(jnp.mean(o * o, axis=-1, keepdims=True) + NORM_EPS)
    return o.reshape(o.shape[0], o.shape[1], -1) * gain.astype(jnp.float32)

def _layer_norm(z, g, b):
    z32 = z.astype(jnp.float32)
    mu = jnp.mean(z32, axis=-1, keepdims=True)
    var = jnp.mean(jnp.square(z32 - mu), axis=-1, keepdims=True)
    out = (z32 - mu) * lax.rsqrt(var + NORM_EPS) * g.astype(jnp.float32) + b.astype(jnp.float32)
    return out.astype(z.dtype)

def _mixer_ab(h, w_in, gate_up, gate_bias, norm_gain, w_out, rel_bias):
    Bsz, S, _ = h.shape
    proj = jnp.einsum('bsd,df->bsf', h, w_in).astype(jnp.float32)
    qa, ka, va, qb, kb, vb, lr_f, lr_b, gate = _split(
        proj, (A_WIDTH, A_WIDTH, A_WIDTH, B_K_WIDTH, B_K_WIDTH, B_V_WIDTH, B_GATE_RANK, B_GATE_RANK, MIX_WIDTH))
    heads = lambda t, n: t.reshape(Bsz, S, n, -1)
    oa = dilated_attention(heads(qa, A_HEADS), heads(ka, A_HEADS), heads(va, A_HEADS), rel_bias)
    oa = oa.reshape(Bsz, S, A_WIDTH)
    up = gate_up.astype(jnp.float32)
    gb_ = gate_bias.astype(jnp.float32)
    g_f = jax.nn.log_sigmoid(lr_f @ up[0] + gb_[0]) / B_GATE_NORMALIZER
    g_b = jax.nn.log_sigmoid(lr_b @ up[1] + gb_[1]) / B_GATE_NORMALIZER
    qh = heads(qb, B_HEADS) * (B_KEY_DIM ** -0.5)
    kh = heads(kb, B_HEADS)
    ob = bidirectional_gated_scan(qh, kh, heads(g_f, B_HEADS), kh, heads(g_b, B_HEADS), heads(vb, B_HEADS))
    ob = _head_rmsnorm(ob, norm_gain)
    y = jnp.concatenate([oa, ob], axis=-1) * jax.nn.silu(gate)
    return jnp.einsum('bsf,fd->bsd', y.astype(h.dtype), w_out)

def _mixer_c(h, w_in, lower_bounds, layer_idx, norm_gain, w_out):
    Bsz, S, _ = h.shape
    proj = jnp.einsum('bsd,df->bsf', h, w_in).astype(jnp.float32)
    q, f_f, f_b, i, gate = _split(proj, (C_WIDTH,) * 5)
    lb = jax.nn.softmax(lower_bounds.astype(jnp.float32), axis=0)
    lb = (jnp.cumsum(lb, axis=0) - lb[0])[layer_idx]
    heads = lambda t: t.reshape(Bsz, S, C_HEADS, C_HEAD_DIM)

    def forget(z):
        f = lb + (1.0 - lb) * jax.nn.sigmoid(z)
        return heads(1.0 - f), heads(jnp.log(f))

    k_f, g_f = forget(f_f)
    k_b, g_b = forget(f_b)
    qh = heads(jax.nn.silu(q)) * (C_HEAD_DIM ** -0.5)
    o = bidirectional_gated_scan(qh, k_f, g_f, k_b, g_b, heads(i))
    y = _head_rmsnorm(o, norm_gain) * jax.nn.silu(gate)
    return jnp.einsum('bsf,fd->bsd', y.astype(h.dtype), w_out)

def first_inputs(seed: int = 0) -> dict:
    key = jax.random.key(seed)
    ks = jax.random.split(key, 13)
    f32 = jnp.float32
    nrm = lambda k, shape, s: jax.random.normal(k, shape, f32) * s
    return {
        'x': nrm(ks[0], (BATCH, SEQ, D_MODEL), 1.0),
        'w_in_ab': nrm(ks[1], (N_EVEN, D_MODEL, AB_IN_WIDTH), D_MODEL ** -0.5),
        'gla_gate_up': nrm(ks[2], (N_EVEN, 2, B_GATE_RANK, B_K_WIDTH), B_GATE_RANK ** -0.5),
        'gla_gate_bias': nrm(ks[3], (N_EVEN, 2, B_K_WIDTH), 0.1),
        'gla_norm': 1.0 + nrm(ks[4], (N_EVEN, B_V_WIDTH), 0.02),
        'w_out_ab': nrm(ks[5], (N_EVEN, MIX_WIDTH, D_MODEL), MIX_WIDTH ** -0.5 * DEEPNORM_BETA),
        'w_in_c': nrm(ks[6], (N_ODD, D_MODEL, C_IN_WIDTH), D_MODEL ** -0.5),
        'hgrn_lower_bounds': nrm(ks[7], (DEPTH, C_WIDTH), 0.1),
        'hgrn_norm': 1.0 + nrm(ks[8], (N_ODD, C_WIDTH), 0.02),
        'w_out_c': nrm(ks[9], (N_ODD, C_WIDTH, D_MODEL), C_WIDTH ** -0.5 * DEEPNORM_BETA),
        'rel_bias': nrm(ks[10], (REL_BUCKETS, A_HEADS), 0.1),
        'ln_gain': 1.0 + nrm(ks[11], (DEPTH, D_MODEL), 0.02),
        'ln_bias': nrm(ks[12], (DEPTH, D_MODEL), 0.02),
    }

def first_block(x, w_in_ab, gla_gate_up, gla_gate_bias, gla_norm, w_out_ab, w_in_c,
              hgrn_lower_bounds, hgrn_norm, w_out_c, rel_bias, ln_gain, ln_bias):
    for layer in range(DEPTH):
        if layer % 2 == 0:
            e = layer // 2
            y = _mixer_ab(x, w_in_ab[e], gla_gate_up[e], gla_gate_bias[e], gla_norm[e], w_out_ab[e], rel_bias)
        else:
            o = layer // 2
            y = _mixer_c(x, w_in_c[o], hgrn_lower_bounds, layer, hgrn_norm[o], w_out_c[o])
        x = _layer_norm(DEEPNORM_ALPHA * x + y, ln_gain[layer], ln_bias[layer])
    return x


DEPTH_2 = 1

GRID_W = 64
CTX_LEN = 256
CHUNK_2 = 64
CONV_W = 5
POOL_WINDOWS = (2, 4, 8, 16)
POOL_DIM = D_MODEL // 4
POOL_GROUP = POOL_DIM // len(POOL_WINDOWS)
SSD_DIM = 3 * D_MODEL // 8
SSD_HEAD_DIM = 64
SSD_HEADS = SSD_DIM // SSD_HEAD_DIM
SSD_GROUPS = 2
SSD_STATE = 128
SSD_BC = SSD_GROUPS * SSD_STATE
GDN_DIM = 3 * D_MODEL // 8
GDN_HEAD_DIM = 64
GDN_HEADS = GDN_DIM // GDN_HEAD_DIM
D_MIX = POOL_DIM + SSD_DIM + GDN_DIM
IN_SPLITS = (POOL_DIM, SSD_DIM, SSD_DIM + 2 * SSD_BC, 2 * SSD_HEADS, 3 * GDN_DIM, GDN_DIM, 2 * GDN_HEADS, 2 * GDN_HEADS)
IN_DIM = sum(IN_SPLITS)
N_EXPERTS = 16
EC_CAPACITY = 2
EXPERT_FF = D_MODEL // 2
EPS = 1e-6
F32 = jnp.float32


def rms_norm(x, g):
    x32 = x.astype(F32)
    y = x32 * lax.rsqrt(jnp.mean(x32 * x32, axis=-1, keepdims=True) + EPS) * g.astype(F32)
    return y.astype(x.dtype)

def l2_norm(a):
    return a * lax.rsqrt(jnp.sum(a * a, axis=-1, keepdims=True) + EPS)

def modulate(h, shift, scale):
    return h * (1 + scale[:, None]) + shift[:, None]

def flip_t(a):
    return jnp.flip(a, axis=1)

def to_column_major(u):
    b, T, C = u.shape
    rows = T // GRID_W
    return u.reshape(b, rows, GRID_W, C).transpose(0, 2, 1, 3).reshape(b, T, C)

def to_raster(u):
    b, T, C = u.shape
    rows = T // GRID_W
    return u.reshape(b, GRID_W, rows, C).transpose(0, 2, 1, 3).reshape(b, T, C)

def to_chunks(a):
    b, T = a.shape[:2]
    a = a.reshape((b, T // CHUNK_2, CHUNK_2) + a.shape[2:])
    return jnp.moveaxis(a, 2, 3)

def dwconv_centred(u, w):
    k, ch = w.shape
    return lax.conv_general_dilated(u, w[:, None, :], window_strides=(1,), padding=[(k // 2, k // 2)],
                                    dimension_numbers=('NWC', 'WIO', 'NWC'), feature_group_count=ch)

def pool_branch(u, pool_w, pool_scale):
    b, T, _ = u.shape
    u32 = u.astype(F32)
    csum = jnp.concatenate([jnp.zeros((b, 1, POOL_DIM), F32), jnp.cumsum(u32, axis=1)], axis=1)
    t = jnp.arange(T)
    groups = []
    for gi, win in enumerate(POOL_WINDOWS):
        lo = jnp.clip(t - win // 2, 0, T)
        hi = jnp.clip(t + win // 2, 0, T)
        sl = slice(gi * POOL_GROUP, (gi + 1) * POOL_GROUP)
        cg = csum[:, :, sl]
        mean = (cg[:, hi] - cg[:, lo]) / (hi - lo).astype(F32)[None, :, None]
        groups.append(mean - u32[:, :, sl])
    d = jnp.stack(groups, axis=2)
    y = jnp.einsum('btgc,gcd->btgd', d, pool_w.astype(F32)).reshape(b, T, POOL_DIM) * pool_scale.astype(F32)
    return y.astype(u.dtype)

def ssd_chunked(xdt, log_a, bm, cm, s0):
    b, T, H, P = xdt.shape
    xc, bc, cc = to_chunks(xdt), to_chunks(bm), to_chunks(cm)
    ac = jnp.cumsum(to_chunks(log_a), axis=-1)
    lower = jnp.tril(jnp.ones((CHUNK_2, CHUNK_2), bool))
    decay = jnp.exp(jnp.where(lower, ac[..., :, None] - ac[..., None, :], -jnp.inf))
    y_intra = jnp.einsum('bchij,bchjp->bchip', jnp.einsum('bchis,bchjs->bchij', cc, bc) * decay, xc)
    states = jnp.einsum('bchjs,bchjp->bchsp', bc * jnp.exp(ac[..., -1:] - ac)[..., None], xc)
    chunk_decay = jnp.exp(ac[..., -1])

    def step(s, inp):
        st, dc = inp
        return s * dc[..., None, None] + st, s

    s_fin, s_start = lax.scan(step, s0, (jnp.moveaxis(states, 1, 0), jnp.moveaxis(chunk_decay, 1, 0)))
    s_start = jnp.moveaxis(s_start, 0, 1)
    y_inter = jnp.einsum('bchis,bchsp->bchip', cc * jnp.exp(ac)[..., None], s_start)
    y = jnp.moveaxis(y_intra + y_inter, 2, 3).reshape(b, T, H, P)
    return y, s_fin

def gdn_chunked(q, k, v, g, beta, s0):
    b, T, H, _ = q.shape
    V = v.shape[-1]
    qc, kc, vc = to_chunks(q), to_chunks(k), to_chunks(v)
    gc = jnp.cumsum(to_chunks(g), axis=-1)
    bc = to_chunks(beta)
    lower = jnp.tril(jnp.ones((CHUNK_2, CHUNK_2), bool))
    strict = jnp.tril(jnp.ones((CHUNK_2, CHUNK_2), bool), -1)
    decay = jnp.exp(jnp.where(lower, gc[..., :, None] - gc[..., None, :], -jnp.inf))
    kb = kc * bc[..., None]
    xm = jnp.where(strict, jnp.einsum('bnhik,bnhjk->bnhij', kb, kc) * decay, 0.0)
    eye = jnp.eye(CHUNK_2, dtype=xm.dtype)
    tm = lax.linalg.triangular_solve(xm + eye, jnp.broadcast_to(eye, xm.shape), left_side=True, lower=True,
                                     unit_diagonal=True)
    u = jnp.einsum('bnhij,bnhjv->bnhiv', tm, vc * bc[..., None])
    w = jnp.einsum('bnhij,bnhjk->bnhik', tm, kb * jnp.exp(gc)[..., None])
    attn = jnp.einsum('bnhik,bnhjk->bnhij', qc, kc) * decay
    qg = qc * jnp.exp(gc)[..., None]
    kend = kc * jnp.exp(gc[..., -1:] - gc)[..., None]
    gend = jnp.exp(gc[..., -1])

    def step(s, inp):
        u_i, w_i, a_i, qg_i, ke_i, ge_i = inp
        v_new = u_i - jnp.einsum('bhlk,bhkv->bhlv', w_i, s)
        o_i = jnp.einsum('bhlk,bhkv->bhlv', qg_i, s) + jnp.einsum('bhij,bhjv->bhiv', a_i, v_new)
        s = s * ge_i[..., None, None] + jnp.einsum('bhlk,bhlv->bhkv', ke_i, v_new)
        return s, o_i

    xs = (jnp.moveaxis(u, 1, 0), jnp.moveaxis(w, 1, 0), jnp.moveaxis(attn, 1, 0),
          jnp.moveaxis(qg, 1, 0), jnp.moveaxis(kend, 1, 0), jnp.moveaxis(gend, 1, 0))
    s_fin, o = lax.scan(step, s0, xs)
    o = jnp.moveaxis(jnp.moveaxis(o, 0, 1), 2, 3).reshape(b, T, H, V)
    return o, s_fin

def ssd_stream(z, xbc, dt_raw, conv_w, conv_b, a_log, dt_bias, d_skip, norm_g, s0_f, s0_b):
    b, T, _ = z.shape
    xbc = jax.nn.silu(dwconv_centred(xbc, conv_w) + conv_b).astype(F32)
    xs, bm, cm = jnp.split(xbc, [SSD_DIM, SSD_DIM + SSD_BC], axis=-1)
    xs = xs.reshape(b, T, SSD_HEADS, SSD_HEAD_DIM)
    rep = SSD_HEADS // SSD_GROUPS
    bm = jnp.repeat(bm.reshape(b, T, SSD_GROUPS, SSD_STATE), rep, axis=2)
    cm = jnp.repeat(cm.reshape(b, T, SSD_GROUPS, SSD_STATE), rep, axis=2)
    dt = jax.nn.softplus(dt_raw.astype(F32).reshape(b, T, 2, SSD_HEADS) + dt_bias.astype(F32))
    a = -jnp.exp(a_log.astype(F32))
    y_f, s_f = ssd_chunked(xs * dt[:, :, 0, :, None], dt[:, :, 0] * a[0], bm, cm, s0_f)
    y_b, s_b = ssd_chunked(flip_t(xs * dt[:, :, 1, :, None]), flip_t(dt[:, :, 1] * a[1]), flip_t(bm), flip_t(cm), s0_b)
    y = y_f + flip_t(y_b) + d_skip.astype(F32)[:, None] * xs
    y = y.reshape(b, T, SSD_DIM) * jax.nn.silu(z.astype(F32))
    return rms_norm(y, norm_g).astype(z.dtype), s_f, s_b

def gdn_stream(qkv, gate, a_raw, b_raw, conv_w, a_log, dt_bias, norm_g, s0_f, s0_b):
    b, T, _ = qkv.shape
    qkv = jax.nn.silu(dwconv_centred(qkv, conv_w)).astype(F32)
    q, k, v = [t.reshape(b, T, GDN_HEADS, GDN_HEAD_DIM) for t in jnp.split(qkv, 3, axis=-1)]
    q = l2_norm(q) * (GDN_HEAD_DIM ** -0.5)
    k = l2_norm(k)
    g = -jnp.exp(a_log.astype(F32)) * jax.nn.softplus(a_raw.astype(F32).reshape(b, T, 2, GDN_HEADS) + dt_bias.astype(F32))
    beta = jax.nn.sigmoid(b_raw.astype(F32).reshape(b, T, 2, GDN_HEADS))
    o_f, s_f = gdn_chunked(q, k, v, g[:, :, 0], beta[:, :, 0], s0_f)
    o_b, s_b = gdn_chunked(flip_t(q), flip_t(k), flip_t(v), flip_t(g[:, :, 1]), flip_t(beta[:, :, 1]), s0_b)
    o = rms_norm(o_f + flip_t(o_b), norm_g).reshape(b, T, GDN_DIM) * jax.nn.silu(gate.astype(F32))
    return o.astype(gate.dtype), s_f, s_b

def hybrid_mixer(h_ctx, h_lat, w_in, w_out, pool_w, pool_scale, ssd_conv_w, ssd_conv_b, ssd_a_log, ssd_dt_bias,
                 ssd_d, ssd_norm_g, gdn_conv_w, gdn_a_log, gdn_dt_bias, gdn_norm_g, with_ctx_out):
    b = h_lat.shape[0]
    cut = np.cumsum(IN_SPLITS)[:-1].tolist()
    pc = jnp.split(h_ctx @ w_in, cut, axis=-1)
    pl = jnp.split(h_lat @ w_in, cut, axis=-1)
    ssd_p = (ssd_conv_w, ssd_conv_b, ssd_a_log, ssd_dt_bias, ssd_d, ssd_norm_g)
    gdn_p = (gdn_conv_w, gdn_a_log, gdn_dt_bias, gdn_norm_g)
    zs = jnp.zeros((b, SSD_HEADS, SSD_STATE, SSD_HEAD_DIM), F32)
    zg = jnp.zeros((b, GDN_HEADS, GDN_HEAD_DIM, GDN_HEAD_DIM), F32)
    s_ctx, ssd_sf, ssd_sb = ssd_stream(pc[1], pc[2], pc[3], *ssd_p, zs, zs)
    g_ctx, gdn_sf, gdn_sb = gdn_stream(pc[4], pc[5], pc[6], pc[7], *gdn_p, zg, zg)
    s_lat, _, _ = ssd_stream(pl[1], pl[2], pl[3], *ssd_p, ssd_sf, ssd_sb)
    g_lat, _, _ = gdn_stream(to_column_major(pl[4]), to_column_major(pl[5]), to_column_major(pl[6]),
                             to_column_major(pl[7]), *gdn_p, gdn_sf, gdn_sb)
    g_lat = to_raster(g_lat)
    lat = jnp.concatenate([pool_branch(pl[0], pool_w, pool_scale), s_lat, g_lat], axis=-1) @ w_out
    if not with_ctx_out:
        return None, lat
    ctx = jnp.concatenate([pool_branch(pc[0], pool_w, pool_scale), s_ctx, g_ctx], axis=-1) @ w_out
    return ctx, lat

def expert_choice_ffn(h, router_w, w_gate, w_up, w_down):
    b, T, D = h.shape
    cap = EC_CAPACITY * T // N_EXPERTS
    aff = jax.nn.softmax(jnp.einsum('btd,de->bte', h.astype(F32), router_w.astype(F32)), axis=-1)
    gate, idx = lax.top_k(jnp.swapaxes(aff, 1, 2), cap)
    xe = jax.vmap(lambda hb, ib: hb[ib])(h, idx)
    hid = jax.nn.silu(jnp.einsum('becd,edf->becf', xe, w_gate)) * jnp.einsum('becd,edf->becf', xe, w_up)
    ye = jnp.einsum('becf,efd->becd', hid, w_down) * gate[..., None].astype(h.dtype)
    return jax.vmap(lambda ib, yb: jnp.zeros((T, D), yb.dtype).at[ib.reshape(-1)].add(yb.reshape(-1, D)))(idx, ye)

def second_inputs(seed: int = 0) -> dict:
    key = jax.random.key(seed)
    ks = iter(jax.random.split(key, 40))

    def nrm(shape, s):
        return jax.random.normal(next(ks), shape, F32) * s

    def gain(shape):
        return 1.0 + nrm(shape, 0.05)

    def dt_bias(shape):
        dt = jnp.exp(jax.random.uniform(next(ks), shape, F32, np.log(1e-3), np.log(1e-1)))
        return dt + jnp.log(-jnp.expm1(-dt))

    def a_log(shape):
        return jnp.log(jax.random.uniform(next(ks), shape, F32, 1.0, 16.0))

    L = DEPTH_2
    return {
        "x": nrm((BATCH, SEQ, D_MODEL), 1.0),
        "c": nrm((BATCH, D_MODEL), 1.0),
        "ctx": nrm((BATCH, CTX_LEN, D_MODEL), 1.0),
        "c_ctx": nrm((D_MODEL,), 1.0),
        "norm1_g": gain((L, D_MODEL)),
        "norm2_g": gain((L, D_MODEL)),
        "ada_w": nrm((L, D_MODEL, 6 * D_MODEL), 0.5 * D_MODEL ** -0.5),
        "ada_b": nrm((L, 6 * D_MODEL), 0.02),
        "w_in": nrm((L, D_MODEL, IN_DIM), D_MODEL ** -0.5),
        "w_out": nrm((L, D_MIX, D_MODEL), D_MIX ** -0.5),
        "pool_w": nrm((L, len(POOL_WINDOWS), POOL_GROUP, POOL_GROUP), POOL_GROUP ** -0.5),
        "pool_scale": gain((L, POOL_DIM)),
        "ssd_conv_w": nrm((L, CONV_W, SSD_DIM + 2 * SSD_BC), CONV_W ** -0.5),
        "ssd_conv_b": nrm((L, SSD_DIM + 2 * SSD_BC), 0.02),
        "ssd_a_log": a_log((L, 2, SSD_HEADS)),
        "ssd_dt_bias": dt_bias((L, 2, SSD_HEADS)),
        "ssd_d": gain((L, SSD_HEADS)),
        "ssd_norm_g": gain((L, SSD_DIM)),
        "gdn_conv_w": nrm((L, CONV_W, 3 * GDN_DIM), CONV_W ** -0.5),
        "gdn_a_log": a_log((L, 2, GDN_HEADS)),
        "gdn_dt_bias": dt_bias((L, 2, GDN_HEADS)),
        "gdn_norm_g": gain((L, GDN_HEAD_DIM)),
        "router_w": nrm((L, D_MODEL, N_EXPERTS), D_MODEL ** -0.5),
        "exp_w_gate": nrm((L, N_EXPERTS, D_MODEL, EXPERT_FF), D_MODEL ** -0.5),
        "exp_w_up": nrm((L, N_EXPERTS, D_MODEL, EXPERT_FF), D_MODEL ** -0.5),
        "exp_w_down": nrm((L, N_EXPERTS, EXPERT_FF, D_MODEL), EXPERT_FF ** -0.5),
        "final_norm_g": gain((D_MODEL,)),
    }

def second_block(x, c, ctx, c_ctx, norm1_g, norm2_g, ada_w, ada_b, w_in, w_out, pool_w, pool_scale, ssd_conv_w,
              ssd_conv_b, ssd_a_log, ssd_dt_bias, ssd_d, ssd_norm_g, gdn_conv_w, gdn_a_log, gdn_dt_bias, gdn_norm_g,
              router_w, exp_w_gate, exp_w_up, exp_w_down, final_norm_g):
    sc = jax.nn.silu(c)
    scc = jax.nn.silu(c_ctx)[None]
    for l in range(DEPTH_2):
        last = l == DEPTH_2 - 1
        m_lat = jnp.split(sc @ ada_w[l] + ada_b[l], 6, axis=-1)
        m_ctx = jnp.split(scc @ ada_w[l] + ada_b[l], 6, axis=-1)
        h_lat = modulate(rms_norm(x, norm1_g[l]), m_lat[0], m_lat[1])
        h_ctx = modulate(rms_norm(ctx, norm1_g[l]), m_ctx[0], m_ctx[1])
        mix_ctx, mix_lat = hybrid_mixer(h_ctx, h_lat, w_in[l], w_out[l], pool_w[l], pool_scale[l], ssd_conv_w[l],
                                        ssd_conv_b[l], ssd_a_log[l], ssd_dt_bias[l], ssd_d[l], ssd_norm_g[l],
                                        gdn_conv_w[l], gdn_a_log[l], gdn_dt_bias[l], gdn_norm_g[l], not last)
        x = x + m_lat[2][:, None] * mix_lat
        h_lat = modulate(rms_norm(x, norm2_g[l]), m_lat[3], m_lat[4])
        x = x + m_lat[5][:, None] * expert_choice_ffn(h_lat, router_w[l], exp_w_gate[l], exp_w_up[l], exp_w_down[l])
        if not last:
            ctx = ctx + m_ctx[2][:, None] * mix_ctx
            h_ctx = modulate(rms_norm(ctx, norm2_g[l]), m_ctx[3], m_ctx[4])
            ctx = ctx + m_ctx[5][:, None] * expert_choice_ffn(h_ctx, router_w[l], exp_w_gate[l], exp_w_up[l],
                                                               exp_w_down[l])
    return rms_norm(x, final_norm_g)


def setup_inputs(seed=0):
    out = dict(first_inputs(seed))
    for name, value in second_inputs(seed + 1).items():
        if name != "x":
            out[name + "_2"] = value
    return out


def reference(
    x, w_in_ab, gla_gate_up, gla_gate_bias, gla_norm, w_out_ab, w_in_c, hgrn_lower_bounds,
    hgrn_norm, w_out_c, rel_bias, ln_gain, ln_bias, c_2, ctx_2, c_ctx_2, norm1_g_2, norm2_g_2,
    ada_w_2, ada_b_2, w_in_2, w_out_2, pool_w_2, pool_scale_2, ssd_conv_w_2, ssd_conv_b_2,
    ssd_a_log_2, ssd_dt_bias_2, ssd_d_2, ssd_norm_g_2, gdn_conv_w_2, gdn_a_log_2, gdn_dt_bias_2,
    gdn_norm_g_2, router_w_2, exp_w_gate_2, exp_w_up_2, exp_w_down_2, final_norm_g_2,
):
    x = first_block(
        x, w_in_ab, gla_gate_up, gla_gate_bias, gla_norm, w_out_ab, w_in_c, hgrn_lower_bounds,
        hgrn_norm, w_out_c, rel_bias, ln_gain, ln_bias,
    )
    return second_block(
        x, c_2, ctx_2, c_ctx_2, norm1_g_2, norm2_g_2, ada_w_2, ada_b_2, w_in_2, w_out_2,
        pool_w_2, pool_scale_2, ssd_conv_w_2, ssd_conv_b_2, ssd_a_log_2, ssd_dt_bias_2, ssd_d_2,
        ssd_norm_g_2, gdn_conv_w_2, gdn_a_log_2, gdn_dt_bias_2, gdn_norm_g_2, router_w_2,
        exp_w_gate_2, exp_w_up_2, exp_w_down_2, final_norm_g_2,
    )


_drawn_inputs = setup_inputs


def setup_inputs(seed=0):
    import zlib

    import numpy as np

    out = dict(_drawn_inputs(seed))
    spreads = {}
    factors = {'gla_gate_up': 2.981,
     'gla_gate_bias': 6.769,
     'gla_norm': 8.0,
     'hgrn_lower_bounds': 8.0,
     'hgrn_norm': 8.0,
     'rel_bias': 8.0,
     'ctx_2': 5.227,
     'c_ctx_2': 7.363,
     'norm1_g_2': 3.071,
     'norm2_g_2': 5.32,
     'pool_scale_2': 6.87,
     'ssd_conv_b_2': 8.0,
     'ssd_d_2': 200.0,
     'ssd_norm_g_2': 5.53,
     'gdn_norm_g_2': 8.0}
    for name, (base, spread) in spreads.items():
        noise = np.random.default_rng([zlib.crc32(name.encode()), seed]).standard_normal(out[name].shape)
        drawn = base * np.exp(spread * noise) if base else spread * noise
        out[name] = __import__('jax').numpy.asarray(drawn.astype(out[name].dtype))
    for name, factor in factors.items():
        out[name] = (out[name] * factor).astype(out[name].dtype)
    return out
```

```python
from contextlib import ExitStack

import numpy as np

import concourse.bass as bass
from concourse import mybir

F32 = mybir.dt.float32
I32 = mybir.dt.int32
U32 = mybir.dt.uint32
ALU = mybir.AluOpType
ACT = mybir.ActivationFunctionType
AX_X = mybir.AxisListType.X

P = 128
D = 1024
KB = D // P
SEQ = 1024
BANK = 512


def wait(eng, sem, value):
    if not isinstance(value, int) or value > 0:
        eng.wait_ge(sem, value)


def own_semaphores(nc, ctx, tag):
    used = []

    def clear():
        nc.clear_and_free_semaphores(used)
        nc.all_engine_barrier()

    def make(name):
        used.append(nc.alloc_semaphore(name=f"{tag}_{name}"))
        return used[-1]

    ctx.callback(clear)
    return make


def make_identity(pool, ident):
    pool.memset(ident[:, :], 0.0)
    pool.drain()
    pool.affine_select(out=ident[:, :], in_=ident[:, :], compare_op=ALU.not_equal, fill=1.0,
                       base=0, pattern=[[-1, P]], channel_multiplier=1)
    pool.drain()


def transpose_in(nc, tag, src, dst, rows):
    T = rows // P
    with ExitStack() as ctx:
        sb = lambda n, s, d=F32: ctx.enter_context(nc.sbuf_tensor(f"{tag}_{n}", s, d))
        sem = own_semaphores(nc, ctx, tag)
        raw = sb("raw", [P, 2, D])
        ident = sb("ident", [P, P])
        ps = [ctx.enter_context(nc.psum_tensor(f"{tag}_ps{b}", [P, BANK], F32)) for b in range(4)]
        ident_ready, turned, copied = sem("ident_ready"), sem("turned"), sem("copied")
        raw_loaded = [sem("raw_loaded0"), sem("raw_loaded1")]
        block = ctx.enter_context(nc.Block())

        @block.gpsimd
        def _(pool):
            make_identity(pool, ident)
            pool.memset(ident[0:1, 0:1], 1.0).then_inc(ident_ready, 1)

        @block.sync
        def _(sp):
            for t in range(T):
                wait(sp, turned, 2 * (t - 1))
                sp.dma_start(raw[:, t % 2, :], src[t * P:(t + 1) * P, :]).then_inc(raw_loaded[t % 2], 16)

        @block.tensor
        def _(pe):
            pe.wait_ge(ident_ready, 1)
            for t in range(T):
                pe.wait_ge(raw_loaded[t % 2], 16 * (t // 2 + 1))
                for h in range(2):
                    n = 2 * t + h
                    wait(pe, copied, n - 3)
                    for j in range(4):
                        last = pe.transpose(ps[n % 4][:, j * P:(j + 1) * P],
                                            raw[:, t % 2, (4 * h + j) * P:(4 * h + j + 1) * P], ident[:, :])
                    last.then_inc(turned, 1)

        @block.vector
        def _(dve):
            for t in range(T):
                for h in range(2):
                    n = 2 * t + h
                    dve.wait_ge(turned, n + 1)
                    dve.tensor_copy(dst[:, 4 * h:4 * h + 4, t * P:(t + 1) * P],
                                    ps[n % 4][:, :].rearrange("p (j c) -> p j c", j=4)).then_inc(copied, 1)


CHANNEL, TOKEN = "channel", "token"


class Job:

    def __init__(self, kind, acts, tokens, weights, col, width, units, dst):
        self.kind, self.acts, self.tokens, self.weights = kind, acts, tokens, weights
        self.col, self.width, self.units, self.dst = col, width, units, dst
        if kind == CHANNEL:
            self.rows = min(width, P)
            self.blocks = width // self.rows
            self.span = min(tokens, BANK)
            self.fills = self.blocks * (tokens // self.span)
            self.staged = self.blocks * tokens
        else:
            self.rows = min(tokens, P)
            tiles = tokens // self.rows
            self.per = min(BANK // width, tiles)
            self.fills = tiles // self.per
            self.staged = tiles * width


def walk(eng, jobs, unit):
    u, f, before = 0, 0, 0
    for job in jobs:
        done = 0
        while done < job.units:
            turns = (job.units - done) // 2
            if done and u >= 4 and f >= 8 and turns > 1 and 2 * job.fills % 8 == 0:
                with eng.Fori(0, turns) as i:
                    for j in range(2):
                        g = f + j * job.fills
                        unit(job, i, u + j, g, g - job.fills, 2 * job.width * i + job.width * (done + j))
                u, f, done = u + 2 * turns, f + 2 * turns * job.fills, done + 2 * turns
                before = f - job.fills
            else:
                unit(job, 0, u, f, before, job.width * done)
                before, u, f, done = f, u + 1, f + job.fills, done + 1
    return u


def project(nc, tag, jobs):
    W = max(j.width for j in jobs)
    with ExitStack() as ctx:
        sb = lambda n, s, d=F32: ctx.enter_context(nc.sbuf_tensor(f"{tag}_{n}", s, d))
        sem = own_semaphores(nc, ctx, tag)
        wbuf = [sb(f"wbuf{b}", [P, KB, W]) for b in range(2)]
        stage = [sb(f"stage{b}", [P, max(j.staged for j in jobs)]) for b in range(2)]
        ps = [ctx.enter_context(nc.psum_tensor(f"{tag}_ps{b}", [P, BANK], F32)) for b in range(8)]
        w_loaded = [sem("w_loaded0"), sem("w_loaded1")]
        stored = [sem("stored0"), sem("stored1")]
        filled, act_moved, dve_moved = sem("filled"), sem("act_moved"), sem("dve_moved")
        block = ctx.enter_context(nc.Block())

        @block.sync
        def _(sp):
            def load(job, i, u, f, before, column):
                if u >= 2:
                    sp.wait_ge(filled, 2 * job.fills * i + before)
                src = job.weights.rearrange("(k p) n -> p k n", p=P)[:, :, bass.ds(job.col + column, job.width)]
                sp.dma_start(wbuf[u % 2][:, :, 0:job.width], src).then_inc(w_loaded[u % 2], 16)

            walk(sp, jobs, load)

        @block.tensor
        def _(pe):
            def multiply(job, i, u, f, before, column):
                wait(pe, w_loaded[u % 2], 16 * i + 16 * (u // 2 + 1))
                w = wbuf[u % 2]
                for n in range(job.fills):
                    g = f + n
                    bank = ps[g % 8]
                    wait(pe, (act_moved, dve_moved)[g % 2], job.fills * i + (g // 2 - 3))
                    if job.kind == CHANNEL:
                        b, s = n % job.blocks, n // job.blocks * job.span
                        for k in range(KB):
                            last = pe.matmul(bank[0:job.rows, 0:job.span], w[:, k, b * job.rows:(b + 1) * job.rows],
                                             job.acts[:, k, s:s + job.span], start=(k == 0), stop=(k == KB - 1))
                    else:
                        for q in range(job.per):
                            t = n * job.per + q
                            for k in range(KB):
                                last = pe.matmul(bank[0:job.rows, q * job.width:(q + 1) * job.width],
                                                 job.acts[:, k, t * P:t * P + job.rows], w[:, k, 0:job.width],
                                                 start=(k == 0), stop=(k == KB - 1))
                    last.then_inc(filled, 1)

            walk(pe, jobs, multiply)

        def move(eng, parity, copy, moved):
            def unit(job, i, u, f, before, column):
                wait(eng, stored[u % 2], 16 * i + 16 * (u // 2))
                for n in range(job.fills):
                    g = f + n
                    if g % 2 != parity:
                        continue
                    eng.wait_ge(filled, 2 * job.fills * i + (g + 1))
                    if job.kind == CHANNEL:
                        b, s = n % job.blocks, n // job.blocks * job.span
                        at = b * job.tokens + s
                        copy(stage[u % 2][0:job.rows, at:at + job.span], ps[g % 8][0:job.rows, 0:job.span]).then_inc(moved, 1)
                    else:
                        m = job.per * job.width
                        copy(stage[u % 2][0:job.rows, n * m:(n + 1) * m], ps[g % 8][0:job.rows, 0:m]).then_inc(moved, 1)
            return unit

        @block.scalar
        def _(act):
            moves = move(act, 0, lambda o, x: act.activation(o, x, ACT.Copy), act_moved)

            def move_and_store(job, i, u, f, before, column):
                moves(job, i, u, f, before, column)
                end = f + job.fills
                act.wait_ge(act_moved, job.fills * i + (end + 1) // 2)
                wait(act, dve_moved, job.fills * i + end // 2)
                if job.kind == CHANNEL:
                    out = job.dst[bass.ds(column, job.width), :].rearrange("(b p) t -> p b t", p=job.rows)
                    src = stage[u % 2][0:job.rows, 0:job.blocks * job.tokens].rearrange("p (b t) -> p b t", b=job.blocks)
                else:
                    out = job.dst[:, bass.ds(column, job.width)].rearrange("(n p) c -> p n c", p=job.rows)
                    src = stage[u % 2][0:job.rows, 0:job.tokens // job.rows * job.width].rearrange("p (n c) -> p n c", c=job.width)
                act.dma_start(out, src).then_inc(stored[u % 2], 16)

            units = walk(act, jobs, move_and_store)
            wait(act, stored[0], 16 * ((units + 1) // 2))
            wait(act, stored[1], 16 * (units // 2))

        @block.vector
        def _(dve):
            walk(dve, jobs, move(dve, 1, lambda o, x: dve.tensor_copy(o, x), dve_moved))


CH = 32
NCH = SEQ // CH
FWD, BWD = 0, 1
TILES = SEQ // P
NEVER = -1e30


def order_masks(pool, mask):
    pool.memset(mask[:, :, :], 1.0)
    pool.drain()
    for d in range(2):
        sign = 1 if d == FWD else -1
        pool.affine_select(out=mask[:, d, :], in_=mask[:, d, :], compare_op=ALU.is_ge, fill=0.0, base=0 if d == FWD else -1,
                           pattern=[[sign, P]], channel_multiplier=-sign)
    pool.drain()


def gated_scan(nc, tag, heads, V, qT, vals, out, *, kT=None, gT=None, g_scale=1.0, zT=None, bounds=None, q_scale=1.0):
    made = zT is not None
    PC = P // CH
    POINTS = PC + 1
    PAIRS = POINTS * PC
    STATES = 2 * (TILES - 1)
    SLOTS = 4
    with ExitStack() as ctx:
        sb = lambda n, s, d=F32: ctx.enter_context(nc.sbuf_tensor(f"{tag}_{n}", s, d))
        sem = own_semaphores(nc, ctx, tag)
        pbank = lambda n: ctx.enter_context(nc.psum_tensor(f"{tag}_{n}", [P, BANK], F32))
        q_in = sb("q_in", [P, 2, SEQ])
        z_in = sb("z_in", [P, 2, 2, SEQ])
        v_in = sb("v_in", [P, 2, TILES, V])
        if made:
            forget = sb("forget", [P, 2, SEQ])
            log_f = sb("log_f", [P, 2, SEQ])
            key = sb("key", [P, 2, SEQ])
            q_act = sb("q_act", [P, SEQ])
            bound_in = sb("bound_in", [P, 2, 2])
            bound_diff = sb("bound_diff", [P, 1])
            low = sb("low", [P, 1])
            room = sb("room", [P, 1])
        else:
            k_in = sb("k_in", [P, 2, SEQ])
        cum = sb("cum", [P, 2, SEQ])
        rel = sb("rel", [P, 2, SEQ])
        grow = sb("grow", [P, 2, SEQ])
        decay = sb("decay", [P, 2, SEQ])
        qd = sb("qd", [P, 2, 2, SEQ])
        kd = sb("kd", [P, 2, 2, SEQ])
        totals = sb("totals", [P, 2, NCH])
        to_mid = sb("to_mid", [P, 2, NCH])
        points = sb("points", [P, 2, TILES * POINTS])
        pairs = sb("pairs", [P, 2, TILES * PAIRS])
        ends = sb("ends", [P, 2, TILES * POINTS])
        end_decay = sb("end_decay", [P, 2, 2, TILES * POINTS])
        pair_decay = sb("pair_decay", [P, 2, 2, TILES * PAIRS])
        starts = sb("starts", [P, 2, SEQ])
        tile_starts = sb("tile_starts", [P, 2, NCH])
        shut = sb("shut", [P, 2, PAIRS])
        mask = sb("mask", [P, 2, P])
        ident = sb("ident", [P, P])
        hold = sb("hold", [1, 2])
        queries = sb("queries", [P, 2, SLOTS, POINTS * P])
        k_end = sb("k_end", [P, 2, 2, P])
        scores = sb("scores", [P, 2, 2, P])
        k_tok = sb("k_tok", [P, 2, 2, P])
        state = sb("state", [P, 2, 2, V])
        o_stage = sb("o_stage", [P, 2, 2, V])
        ps_scores = [pbank("ps_scores0"), pbank("ps_scores1")]
        ps_keys = [pbank("ps_keys0"), pbank("ps_keys1")]
        ps_upd = [pbank("ps_upd0"), pbank("ps_upd1")]
        ps_out = [pbank(f"out{d}") for d in range(2)]

        LOADS = 5
        loaded = [sem("loaded0"), sem("loaded1")]
        consts = sem("consts")
        diff_done, q_act_done = sem("diff_done"), sem("q_act_done")
        sig_done, f_done, ln_done, key_done = sem("sig_done"), sem("f_done"), sem("ln_done"), sem("key_done")
        rel_done, points_done, exps_done, decay_done = sem("rel_done"), sem("points_done"), sem("exps_done"), sem("decay_done")
        q_done, k_done = sem("q_done"), sem("k_done")
        turned, scored, scores_done, ktok_done = sem("turned"), sem("scored"), sem("scores_done"), sem("ktok_done")
        queries_done, k_end_done = sem("queries_done"), sem("k_end_done")
        upd_done, state_done = sem("upd_done"), sem("state_done")
        out_done, out_moved = sem("out_done"), sem("out_moved")
        stored = [[sem(f"stored{d}{b}") for b in range(2)] for d in range(2)]
        block = ctx.enter_context(nc.Block())

        def at(i, j, count, more):
            return 2 * count * i + (count * j + more)

        def tile_of(p, d):
            return p if d == FWD else TILES - 1 - p

        def walk_heads(eng, head):
            head(0, 0)
            head(0, 1)
            if heads > 4:
                with eng.Fori(1, heads // 2 - 1) as i:
                    head(i, 0)
                    head(i, 1)
            head(0, heads - 2)
            head(0, heads - 1)

        def is_last(i, j):
            return isinstance(i, int) and j == heads - 1

        @block.sync
        def _(sp):
            def load(i, j):
                b = j % 2
                rows = lambda t: t[bass.ds(2 * P * i + P * j, P), :]
                wait(sp, k_done, at(i, j - 2, 2, 2))
                wait(sp, q_done, at(i, j - 2, 2, 2))
                wait(sp, out_done, at(i, j - 2, 16, 16))
                sp.dma_start(q_in[:, b, :], rows(qT)).then_inc(loaded[b], 16)
                if made:
                    sp.dma_start(bound_in[:, b, :], bounds[bass.ds(2 * P * i + P * j, P), :]).then_inc(loaded[b], 16)
                else:
                    sp.dma_start(k_in[:, b, :], rows(kT)).then_inc(loaded[b], 16)
                for d in range(2):
                    sp.dma_start(z_in[:, b, d, :], rows((zT if made else gT)[d])).then_inc(loaded[b], 16)
                sp.dma_start(v_in[:, b, :, :], vals[:, bass.ds(2 * V * i + V * j, V)].rearrange("(t p) v -> p t v", p=P)).then_inc(loaded[b], 16)

            load(0, 0)
            load(0, 1)

            def head(i, j):
                for p in range(TILES):
                    for d in range(2):
                        sp.wait_ge(out_moved, at(i, j, 16, 2 * p + d + 1))
                        t = tile_of(p, d)
                        sp.dma_start(out[d][t * P:(t + 1) * P, bass.ds(2 * V * i + V * j, V)],
                                     o_stage[:, d, p % 2, :]).then_inc(stored[d][p % 2], 16)
                if not isinstance(i, int) or j + 2 < heads:
                    load(i, j + 2)
            walk_heads(sp, head)
            for d in range(2):
                for b in range(2):
                    sp.wait_ge(stored[d][b], 16 * heads * TILES // 2)

        @block.gpsimd
        def _(pool):
            make_identity(pool, ident)
            order_masks(pool, mask)
            pool.memset(starts[:, :, :], 1.0)
            pool.memset(tile_starts[:, :, :], 1.0)
            pool.memset(shut[:, :, :], 0.0)
            pool.memset(scores[:, :, :, :], 0.0)
            pool.drain()
            pool.memset(points[:, :, PC::POINTS], 0.0)
            for c in range(PC):
                if c:
                    pool.memset(shut[:, FWD, PC * c:PC * c + c], NEVER)
                if c + 1 < PC:
                    pool.memset(shut[:, BWD, PC * c + c + 1:PC * (c + 1)], NEVER)
            pool.memset(tile_starts[:, 0, 0::PC], 0.0)
            pool.memset(tile_starts[:, 1, PC - 1::PC], 0.0)
            pool.memset(starts[:, 0, 0::CH], 0.0)
            pool.memset(starts[:, 1, CH - 1::CH], 0.0)
            pool.drain()
            pool.memset(ident[0:1, 0:1], 1.0).then_inc(consts, 1)

            def prepare(i, j, piece):
                b = j % 2
                if piece in (6, 7):
                    d = piece - 6
                    pool.drain()
                    pool.wait_ge(exps_done, at(i, j, 4, 2 * d + 2))
                    wait(pool, out_done, at(i, j - 2, 16, 16))
                    k = key[:, d, :] if made else k_in[:, b, :]
                    pool.tensor_tensor(kd[:, b, d, :], k, decay[:, d, :], ALU.mult).then_inc(k_done, 1)

            def scale_queries(i, j, p):
                b = j % 2
                pool.drain()
                for d in range(2):
                    t = tile_of(p, d)
                    if p == 0:
                        pool.wait_ge(decay_done, at(i, j, 2, d + 1))
                        pool.wait_ge(q_done, at(i, j, 2, d + 1))
                    wait(pool, out_done, at(i, j, 2 * TILES, 2 * (p - SLOTS) + d + 1))
                    q = qd[:, b, d, t * P:(t + 1) * P].rearrange("p (o a c) -> p o a c", o=1, a=PC).to_broadcast([P, POINTS, PC, CH])
                    f = pair_decay[:, b, d, t * PAIRS:(t + 1) * PAIRS].rearrange("p (b a o) -> p b a o", a=PC, o=1).to_broadcast([P, POINTS, PC, CH])
                    pool.tensor_tensor(queries[:, d, p % SLOTS, :].rearrange("p (b a c) -> p b a c", b=POINTS, a=PC), q, f, ALU.mult).then_inc(queries_done, 1)

            for piece in range(8):
                prepare(0, 0, piece)

            def head(i, j):
                for p in range(TILES):
                    scale_queries(i, j, p)
                    if not is_last(i, j):
                        prepare(i, j + 1, p)
            walk_heads(pool, head)

        @block.tensor
        def _(pe):
            def front(i, j, p):
                b = j % 2
                if p == 0:
                    pe.wait_ge(k_done, at(i, j, 2, 2))
                pe.wait_ge(queries_done, at(i, j, 2 * TILES, 2 * p + 2))
                wait(pe, scores_done, at(i, j, 2 * TILES, 2 * (p - 1)))
                for d in range(2):
                    for c in range(PC):
                        rows = slice(c * CH, (c + 1) * CH)
                        first = tile_of(p, d) * P + c * CH
                        lo, hi = (c * CH, P) if d == FWD else (0, (c + 1) * CH)
                        last = pe.matmul(ps_scores[p % 2][rows, d * P + lo:d * P + hi], kd[:, b, d, first:first + CH],
                                         queries[:, d, p % SLOTS, c * P + lo:c * P + hi], start=True, stop=True, skip_group_check=True)
                last.then_inc(scored, 1)
                pe.wait_ge(k_end_done, at(i, j, 2 * TILES, 2 * p + 2))
                wait(pe, ktok_done, at(i, j, 2 * TILES, 2 * (p - 1)))
                for d in range(2):
                    last = pe.transpose(ps_keys[p % 2][:, d * P:(d + 1) * P], k_end[:, d, p % 2, :], ident[:, :])
                last.then_inc(turned, 1)

            def update(i, j, p):
                b = j % 2
                pe.wait_ge(ktok_done, at(i, j, 2 * TILES, 2 * p + 2))
                wait(pe, state_done, at(i, j, STATES, max(0, 2 * (p - 1))))
                for d in range(2):
                    last = pe.matmul(ps_upd[p % 2][:, d * V:(d + 1) * V], k_tok[:, d, p % 2, :], v_in[:, b, tile_of(p, d), :],
                                     start=True, stop=True, skip_group_check=True)
                last.then_inc(upd_done, 1)

            def output(i, j, p):
                b = j % 2
                for d in range(2):
                    pe.wait_ge(scores_done, at(i, j, 2 * TILES, 2 * p + d + 1))
                    wait(pe, out_moved, at(i, j, 2 * TILES, 2 * p + d - 1))
                    last = pe.matmul(ps_out[d][:, 0:V], scores[:, d, p % 2, :], v_in[:, b, tile_of(p, d), :],
                                     start=True, stop=(p == 0), skip_group_check=True)
                    if p:
                        pe.wait_ge(state_done, at(i, j, STATES, 2 * (p - 1) + d + 1))
                        last = pe.matmul(ps_out[d][:, 0:V], queries[:, d, p % SLOTS, PC * P:POINTS * P], state[:, d, p % 2, :],
                                         start=False, stop=True, skip_group_check=True)
                    last.then_inc(out_done, 1)

            def head(i, j):
                pe.wait_ge(loaded[j % 2], 16 * LOADS * i + 16 * LOADS * (j // 2 + 1))
                front(i, j, 0)
                for p in range(TILES):
                    if p < TILES - 1:
                        front(i, j, p + 1)
                        update(i, j, p)
                    output(i, j, p)

            pe.wait_ge(consts, 1)
            for b in range(2):
                for d in range(2):
                    pe.transpose(ps_scores[b][:, d * P:(d + 1) * P], ident[:, :], ident[:, :])
            walk_heads(pe, head)

        @block.vector
        def _(dve):
            def prepare(i, j, piece):
                b = j % 2
                if made and piece == 0:
                    dve.wait_ge(loaded[b], 16 * LOADS * i + 16 * LOADS * (j // 2 + 1))
                    wait(dve, sig_done, at(i, j, 2, 0))
                    dve.tensor_tensor(bound_diff[:, :], bound_in[:, b, 1:2], bound_in[:, b, 0:1], ALU.subtract).then_inc(diff_done, 1)
                if made and piece == 1:
                    dve.wait_ge(sig_done, at(i, j, 2, 1))
                    dve.tensor_scalar(room[:, :], low[:, :], -1.0, 1.0, ALU.mult, ALU.add)
                    dve.drain()
                    for d in range(2):
                        dve.wait_ge(sig_done, at(i, j, 2, d + 1))
                        dve.tensor_scalar(forget[:, d, :], forget[:, d, :], room[:, 0:1], low[:, 0:1], ALU.mult, ALU.add).then_inc(f_done, 1)
                    dve.drain()
                    for d in range(2):
                        wait(dve, k_done, at(i, j, 2, 0))
                        dve.tensor_scalar(key[:, d, :], forget[:, d, :], -1.0, 1.0, ALU.mult, ALU.add).then_inc(key_done, 1)
                if piece in (3, 4):
                    d = piece - 3
                    if made:
                        dve.wait_ge(ln_done, at(i, j, 2, d + 1))
                    else:
                        dve.wait_ge(loaded[b], 16 * LOADS * i + 16 * LOADS * (j // 2 + 1))
                    g = log_f[:, d, :] if made else z_in[:, b, d, :]
                    step = 1 if d == FWD else -1
                    dve.tensor_tensor_scan(cum[:, d, ::step], starts[:, d, ::step], g[:, ::step], 0.0, ALU.mult, ALU.add)
                    dve.drain()
                    chunks = cum[:, d, :].rearrange("p (n t) -> p n t", t=CH)
                    mid = CH // 2 - 1 if d == FWD else CH // 2
                    end = CH - 1 if d == FWD else 0
                    wait(dve, exps_done, at(i, j, 4, 0))
                    wait(dve, decay_done, at(i, j, 2, 0))
                    dve.tensor_tensor(rel[:, d, :].rearrange("p (n t) -> p n t", t=CH), chunks,
                                      chunks[:, :, mid:mid + 1].to_broadcast([P, NCH, CH]), ALU.subtract).then_inc(rel_done, 1)
                    dve.tensor_tensor(to_mid[:, d, :], chunks[:, :, mid], chunks[:, :, end], ALU.subtract)
                    dve.tensor_tensor_scan(totals[:, d, ::step], tile_starts[:, d, ::step], chunks[:, ::step, end], 0.0, ALU.mult, ALU.add)
                    dve.drain()
                    m = points[:, d, :].rearrange("p (t a) -> p t a", a=POINTS)
                    per_tile = lambda x: x[:, d, :].rearrange("p (t c) -> p t c", c=PC)
                    whole = per_tile(totals)[:, :, PC - 1:PC] if d == FWD else per_tile(totals)[:, :, 0:1]
                    to_end = ends[:, d, :].rearrange("p (t a) -> p t a", a=POINTS)
                    dve.tensor_tensor(m[:, :, 0:PC], per_tile(totals), per_tile(to_mid), ALU.add)
                    dve.tensor_copy(to_end[:, :, PC:POINTS], whole)
                    dve.drain()
                    dve.tensor_tensor(to_end[:, :, 0:PC], whole.to_broadcast([P, TILES, PC]), m[:, :, 0:PC], ALU.subtract)
                    shape = [P, TILES, POINTS, PC]
                    m_b = points[:, d, :].rearrange("p (t b o) -> p t b o", b=POINTS, o=1).to_broadcast(shape)
                    m_a = points[:, d, :].rearrange("p (t o a) -> p t o a", a=POINTS, o=1)[:, :, :, 0:PC].to_broadcast(shape)
                    dve.tensor_tensor(pairs[:, d, :].rearrange("p (t b a) -> p t b a", b=POINTS, a=PC), m_a, m_b, ALU.subtract)
                    dve.drain()
                    per_pair = pairs[:, d, :].rearrange("p (t x) -> p t x", x=PAIRS)
                    dve.tensor_tensor(per_pair, per_pair, shut[:, d, :].rearrange("p (o x) -> p o x", o=1).to_broadcast([P, TILES, PAIRS]),
                                      ALU.add).then_inc(points_done, 1)
                if piece in (6, 7):
                    d = piece - 6
                    dve.wait_ge(exps_done, at(i, j, 4, 2 * d + 1))
                    if made:
                        dve.wait_ge(q_act_done, at(i, j, 1, 1))
                    wait(dve, out_done, at(i, j - 2, 16, 16))
                    q = q_act[:, :] if made else q_in[:, b, :]
                    dve.scalar_tensor_tensor(out=qd[:, b, d, :], in0=q, scalar=q_scale, in1=grow[:, d, :],
                                             op0=ALU.mult, op1=ALU.mult).then_inc(q_done, 1)

            def pick(i, j, p):
                dve.drain()
                dve.wait_ge(scored, at(i, j, 8, p + 1))
                for d in range(2):
                    wait(dve, out_done, at(i, j, 16, 2 * p + d - 3))
                    dve.memset(hold[:, d:d + 1], 0.0)
                    dve.copy_predicated(scores[:, d, p % 2, :], mask[:, d, :].bitcast(U32), ps_scores[p % 2][:, d * P:(d + 1) * P]).then_inc(scores_done, 1)

            def scale_keys(i, j, p):
                b = j % 2
                dve.drain()
                for d in range(2):
                    t = tile_of(p, d)
                    if p == 0:
                        dve.wait_ge(decay_done, at(i, j, 2, d + 1))
                        dve.wait_ge(k_done, at(i, j, 2, d + 1))
                    wait(dve, turned, at(i, j, TILES, p - 1))
                    f = end_decay[:, b, d, t * POINTS:t * POINTS + PC].rearrange("p (a o) -> p a o", o=1).to_broadcast([P, PC, CH])
                    dve.tensor_tensor(k_end[:, d, p % 2, :].rearrange("p (a c) -> p a c", c=CH),
                                      kd[:, b, d, t * P:(t + 1) * P].rearrange("p (a c) -> p a c", c=CH), f, ALU.mult).then_inc(k_end_done, 1)

            def carry_on(i, j, p):
                b = j % 2
                dve.drain()
                dve.wait_ge(upd_done, at(i, j, TILES - 1, p + 1))
                for d in range(2):
                    wait(dve, out_done, at(i, j, 2 * TILES, 2 * p + d - 1))
                    add = ps_upd[p % 2][:, d * V:(d + 1) * V]
                    new = state[:, d, (p + 1) % 2, :]
                    if p == 0:
                        dve.tensor_copy(new, add).then_inc(state_done, 1)
                    else:
                        end = tile_of(p, d) * POINTS + PC
                        dve.scalar_tensor_tensor(out=new, in0=state[:, d, p % 2, :], scalar=end_decay[:, b, d, end:end + 1],
                                                 in1=add, op0=ALU.mult, op1=ALU.add).then_inc(state_done, 1)

            def head(i, j):
                scale_keys(i, j, 0)
                pick(i, j, 0)
                for p in range(TILES):
                    if p < TILES - 1:
                        scale_keys(i, j, p + 1)
                        pick(i, j, p + 1)
                        carry_on(i, j, p)
                    if not is_last(i, j):
                        prepare(i, j + 1, p)

            dve.wait_ge(consts, 1)
            for piece in range(8):
                prepare(0, 0, piece)
            walk_heads(dve, head)

        @block.scalar
        def _(act):
            def prepare(i, j, piece):
                b = j % 2
                if made and piece == 0:
                    act.wait_ge(loaded[b], 16 * LOADS * i + 16 * LOADS * (j // 2 + 1))
                    act.wait_ge(diff_done, at(i, j, 1, 1))
                    wait(act, f_done, at(i, j, 2, 0))
                    act.activation(low[:, :], bound_diff[:, :], ACT.Sigmoid)
                    act.drain()
                    wait(act, key_done, at(i, j, 2, 0))
                    act.activation(forget[:, 0, :], z_in[:, b, 0, :], ACT.Sigmoid).then_inc(sig_done, 1)
                if made and piece == 1:
                    act.activation(forget[:, 1, :], z_in[:, b, 1, :], ACT.Sigmoid).then_inc(sig_done, 1)
                if made and piece == 3:
                    wait(act, q_done, at(i, j, 2, 0))
                    act.activation(q_act[:, :], q_in[:, b, :], ACT.Silu).then_inc(q_act_done, 1)
                if made and piece == 2:
                    for d in range(2):
                        act.wait_ge(f_done, at(i, j, 2, d + 1))
                        wait(act, rel_done, at(i, j, 2, 0))
                        act.activation(log_f[:, d, :], forget[:, d, :], ACT.Ln).then_inc(ln_done, 1)
                if piece in (4, 5):
                    d = piece - 4
                    act.wait_ge(rel_done, at(i, j, 2, d + 1))
                    wait(act, q_done, at(i, j, 2, 0))
                    wait(act, k_done, at(i, j, 2, 0))
                    act.activation(grow[:, d, :], rel[:, d, :], ACT.Exp, scale=g_scale).then_inc(exps_done, 1)
                    act.activation(decay[:, d, :], rel[:, d, :], ACT.Exp, scale=-g_scale).then_inc(exps_done, 1)
                    act.wait_ge(points_done, at(i, j, 2, d + 1))
                    act.activation(end_decay[:, b, d, :], ends[:, d, :], ACT.Exp, scale=g_scale)
                    act.activation(pair_decay[:, b, d, :], pairs[:, d, :], ACT.Exp, scale=g_scale).then_inc(decay_done, 1)

            def move_keys(i, j, p):
                act.wait_ge(turned, at(i, j, 8, p + 1))
                for d in range(2):
                    wait(act, out_done, at(i, j, 16, 2 * p + d - 3))
                    act.activation(k_tok[:, d, p % 2, :], ps_keys[p % 2][:, d * P:(d + 1) * P], ACT.Copy).then_inc(ktok_done, 1)

            def move_out(i, j, p):
                for d in range(2):
                    act.wait_ge(out_done, at(i, j, 16, 2 * p + d + 1))
                    wait(act, stored[d][p % 2], at(i, j, 64, 16 * (p // 2)))
                    act.activation(o_stage[:, d, p % 2, :], ps_out[d][:, 0:V], ACT.Copy).then_inc(out_moved, 1)

            def head(i, j):
                act.drain()
                move_keys(i, j, 0)
                for p in range(TILES):
                    if p < TILES - 1:
                        move_keys(i, j, p + 1)
                    if p > 0:
                        move_out(i, j, p - 1)
                    if not is_last(i, j):
                        prepare(i, j + 1, p)
                move_out(i, j, TILES - 1)

            for piece in range(8):
                prepare(0, 0, piece)
            walk_heads(act, head)


EPS1 = 1e-5


def row_to_all(vector, n):
    return vector.rearrange("(a n) -> a n", a=1).to_broadcast([P, n])


def close_layer(nc, tag, x, x_next, xT_next, o, gate, gain, w_out, ln_gain, ln_bias, V, alpha, attn=None, attn_heads=0):
    WO = o[0].shape[1]
    H = WO // V
    A = attn_heads * 64
    W = A + WO
    NB = W // P
    PAIR = P + 4
    AR = PAIR * attn_heads // 2
    two = lambda t: t.rearrange("p (g h) -> p g h", h=2)
    T = SEQ // P
    with ExitStack() as ctx:
        sb = lambda n, s, d=F32: ctx.enter_context(nc.sbuf_tensor(f"{tag}_{n}", s, d))
        sem = own_semaphores(nc, ctx, tag)
        pbank = lambda n: ctx.enter_context(nc.psum_tensor(f"{tag}_{n}", [P, BANK], F32))
        w = sb("w", [P, NB, D])
        gains = sb("gains", [P, WO])
        lng, lnb = sb("lng", [P, D]), sb("lnb", [P, D])
        ident = sb("ident", [P, P])
        of, ob = sb("of", [P, 2, WO]), sb("ob", [P, WO])
        gt = sb("gt", [P, 2, W])
        xt = sb("xt", [P, 2, D])
        y = sb("y", [P, W])
        yT = sb("yT", [P, NB, P])
        z = sb("z", [P, D])
        xn = sb("xn", [P, 2, D])
        squares = sb("squares", [P, WO])
        ss, std, rstd = sb("ss", [P, H]), sb("std", [P, H]), sb("rstd", [P, H])
        bn, mv = sb("bn", [P, 2, 6]), sb("mv", [P, 2])
        lstd, lrstd = sb("lstd", [P, 1]), sb("lrstd", [P, 1])
        eps = sb("eps", [P, 1])
        if attn is not None:
            NA = 3
            parts = sb("parts", [P, NA, AR])
            top = sb("top", [P, attn_heads])
            lift, den = sb("lift", [P, NA, attn_heads]), sb("den", [P, NA, attn_heads])
            merged = sb("merged", [P, A])
        ps_y = [pbank(f"ps_y{n}") for n in range(3)]
        ps_z = [pbank(f"ps_z{n}") for n in range(2)]
        ps_x = [pbank(f"ps_x{n}") for n in range(2)]

        vec_loaded, w_loaded, consts = sem("vec_loaded"), sem("w_loaded"), sem("consts")
        LOADS = 3 if attn is None else 4
        loaded = [sem("loaded0"), sem("loaded1")]
        x_loaded = [sem("x_loaded0"), sem("x_loaded1")]
        summed, squared, gated = sem("summed"), sem("squared"), sem("gated")
        var_done, std_done, normed, y_done = sem("var_done"), sem("std_done"), sem("normed"), sem("y_done")
        y_turned, y_moved, z_made, z_moved = sem("y_turned"), sem("y_moved"), sem("z_made"), sem("z_moved")
        lvar_done, lstd_done, centred, x_done = sem("lvar_done"), sem("lstd_done"), sem("centred"), sem("x_done")
        x_turned, x_moved = sem("x_turned"), sem("x_moved")
        stored = [sem("stored0"), sem("stored1")]
        lift_in, lift_out = sem("lift_in"), sem("lift_out")
        block = ctx.enter_context(nc.Block())

        def after(i, b):
            return (i, 1) if b == 0 else (i + 1, 0)

        def before(i, b):
            return (i, 0) if b == 1 else (i - 1, 1)

        def tiles(eng, slot):
            slot(0, 0, True, False)
            slot(0, 1, False, False)
            with eng.Fori(1, T // 2 - 1) as i:
                slot(i, 0, False, False)
                slot(i, 1, False, False)
            slot(T // 2 - 1, 0, False, False)
            slot(T // 2 - 1, 1, False, True)

        def rows(i, b):
            return bass.ds(2 * P * i + P * b, P)

        @block.sync
        def _(sp):
            def load(i, b):
                wait(sp, y_done, 2 * i + b)
                sp.dma_start(of[:, b, :], o[0][rows(i, b), :]).then_inc(loaded[b], 16)
                sp.dma_start(ob[:, :], o[1][rows(i, b), :]).then_inc(loaded[b], 16)
                sp.dma_start(gt[:, b, :], gate[rows(i, b), :]).then_inc(loaded[b], 16)
                if attn is not None:
                    sp.dma_start(parts[:, :, :], attn[:, rows(i, b), :].rearrange("a p n -> p a n")).then_inc(loaded[b], 16)

            def load_x(i, b):
                wait(sp, z_moved, 2 * i + (b - 1))
                sp.dma_start(xt[:, b, :], x[rows(i, b), :]).then_inc(x_loaded[b], 16)

            load(0, 0)
            for dst, src in ((gains, gain), (lng, ln_gain), (lnb, ln_bias)):
                sp.dma_start(dst[:, :], row_to_all(src, dst.shape[1])).then_inc(vec_loaded, 16)
            sp.dma_start(w[:, :, :], w_out.rearrange("(k p) n -> p k n", p=P)).then_inc(w_loaded, 16)
            load_x(0, 0)
            load(0, 1)
            load_x(0, 1)

            def slot(i, b, first, last):
                if not last and not (isinstance(i, int) and 2 * i + b + 2 >= T):
                    load(i + 1, b)
                    load_x(i + 1, b)
                sp.wait_ge(x_done, 2 * i + b + 1)
                sp.dma_start(x_next[rows(i, b), :], xn[:, b, :]).then_inc(stored[b], 16)
            tiles(sp, slot)
            sp.wait_ge(stored[0], 8 * T)
            sp.wait_ge(stored[1], 8 * T)

        @block.gpsimd
        def _(pool):
            make_identity(pool, ident)
            pool.memset(eps[:, :], EPS1)
            pool.drain()
            pool.memset(ident[0:1, 0:1], 1.0).then_inc(consts, 1)

            def front(i, b):
                n = 2 * i + b
                pool.wait_ge(loaded[b], 16 * LOADS * i + 16 * LOADS)
                pool.tensor_tensor(of[:, b, :], of[:, b, :], ob[:, :], ALU.add).then_inc(summed, 1)
                pool.wait_ge(normed, n + 1)
                pool.wait_ge(gated, n + 1)
                pool.tensor_tensor(y[:, :], y[:, :], gt[:, b, :], ALU.mult).then_inc(y_done, 1)

            def slot(i, b, first, last):
                if not last:
                    front(*after(i, b))
                pool.wait_ge(centred, 2 * i + b + 1)
                wait(pool, stored[b], 16 * i)
                wait(pool, x_turned, 4 * i + (2 * b - 2))
                pool.tensor_tensor(xn[:, b, :], z[:, :], lng[:, :], ALU.mult)
                pool.drain()
                pool.tensor_tensor(xn[:, b, :], xn[:, b, :], lnb[:, :], ALU.add).then_inc(x_done, 1)

            front(0, 0)
            tiles(pool, slot)

        @block.scalar
        def _(act):
            act.wait_ge(consts, 1)

            def front(i, b):
                n = 2 * i + b
                act.wait_ge(loaded[b], 16 * LOADS * i + 16 * LOADS)
                if attn is not None:
                    act.wait_ge(lift_in, n + 1)
                    act.activation(lift[:, :, :], lift[:, :, :], ACT.Exp, scale=0.125).then_inc(lift_out, 1)
                act.activation(gt[:, b, :], gt[:, b, :], ACT.Silu).then_inc(gated, 1)
                act.wait_ge(summed, n + 1)
                wait(act, var_done, n)
                for h in range(H):
                    last = act.activation(squares[:, h * V:(h + 1) * V], of[:, b, h * V:(h + 1) * V], ACT.Square, accum_out=ss[:, h:h + 1])
                last.then_inc(squared, 1)
                act.wait_ge(var_done, n + 1)
                act.activation(std[:, :], rstd[:, :], ACT.Sqrt).then_inc(std_done, 1)

            def move_y(i, b):
                n = 2 * i + b
                for g in range(NB // 4):
                    act.wait_ge(y_turned, 3 * n + g + 1)
                    wait(act, z_made, n)
                    act.activation(yT[:, 4 * g:4 * g + 4, :], ps_y[g][:, :].rearrange("p (j c) -> p j c", j=4), ACT.Copy).then_inc(y_moved, 1)

            def move_x(i, b):
                for h in range(2):
                    act.wait_ge(x_turned, 4 * i + 2 * b + h + 1)
                    act.activation(xT_next[:, 4 * h:4 * h + 4, rows(i, b)],
                                   ps_x[h][:, :].rearrange("p (j c) -> p j c", j=4), ACT.Copy).then_inc(x_moved, 1)

            def slot(i, b, first, last):
                if not last:
                    front(*after(i, b))
                    move_y(*after(i, b))
                act.wait_ge(lvar_done, 2 * i + b + 1)
                act.activation(lstd[:, :], mv[:, 1:2], ACT.Sqrt, bias=eps[:, 0:1]).then_inc(lstd_done, 1)
                if not first:
                    move_x(*before(i, b))

            front(0, 0)
            move_y(0, 0)
            tiles(act, slot)
            move_x(T // 2 - 1, 1)

        @block.tensor
        def _(pe):
            pe.wait_ge(consts, 1)

            def turn_y(i, b):
                n = 2 * i + b
                pe.wait_ge(y_done, n + 1)
                for g in range(NB // 4):
                    wait(pe, y_moved, 3 * n)
                    for j in range(4):
                        k = 4 * g + j
                        last = pe.transpose(ps_y[g][:, j * P:(j + 1) * P], y[:, k * P:(k + 1) * P], ident[:, :])
                    last.then_inc(y_turned, 1)

            def turn_x(i, b):
                pe.wait_ge(x_done, 2 * i + b + 1)
                wait(pe, x_moved, 4 * i + 2 * b)
                for h in range(2):
                    for j in range(4):
                        last = pe.transpose(ps_x[h][:, j * P:(j + 1) * P], xn[:, b, (4 * h + j) * P:(4 * h + j + 1) * P], ident[:, :])
                    last.then_inc(x_turned, 1)

            def slot(i, b, first, last):
                n = 2 * i + b
                pe.wait_ge(y_moved, 3 * n + 3)
                wait(pe, z_moved, n)
                for h in range(2):
                    for k in range(NB):
                        made = pe.matmul(ps_z[h][:, :], yT[:, k, :], w[:, k, h * BANK:(h + 1) * BANK],
                                         start=(k == 0), stop=(k == NB - 1))
                made.then_inc(z_made, 1)
                if not last:
                    turn_y(*after(i, b))
                if not first:
                    turn_x(*before(i, b))

            turn_y(0, 0)
            pe.wait_ge(w_loaded, 16)
            tiles(pe, slot)
            turn_x(T // 2 - 1, 1)

        @block.vector
        def _(dve):
            dve.wait_ge(consts, 1)

            def front(i, b):
                n = 2 * i + b
                dve.drain()
                dve.wait_ge(loaded[b], 16 * LOADS * i + 16 * LOADS)
                wait(dve, y_turned, 3 * n)
                if attn is not None:
                    pairs = parts[:, :, :].rearrange("p a (g c) -> p a g c", c=PAIR)
                    m, sums = pairs[:, :, :, P:P + 2], pairs[:, :, :, P + 2:P + 4]
                    dve.tensor_tensor(two(top[:, :]), m[:, 0], m[:, 1], ALU.max)
                    dve.drain()
                    dve.tensor_tensor(two(top[:, :]), two(top[:, :]), m[:, 2], ALU.max)
                    dve.drain()
                    for a in range(NA):
                        last = dve.tensor_tensor(two(lift[:, a, :]), m[:, a], two(top[:, :]), ALU.subtract)
                    last.then_inc(lift_in, 1)
                    dve.wait_ge(lift_out, n + 1)
                    for a in range(NA):
                        dve.tensor_tensor(two(den[:, a, :]), two(lift[:, a, :]), sums[:, a], ALU.mult)
                    dve.drain()
                    dve.tensor_tensor(den[:, 0, :], den[:, 0, :], den[:, 1, :], ALU.add)
                    dve.drain()
                    dve.tensor_tensor(den[:, 0, :], den[:, 0, :], den[:, 2, :], ALU.add)
                    dve.drain()
                    dve.reciprocal(den[:, 1, :], den[:, 0, :])
                    dve.drain()
                    for a in range(NA):
                        dve.tensor_tensor(lift[:, a, :], lift[:, a, :], den[:, 1, :], ALU.mult)
                    dve.drain()
                    for a in range(NA):
                        out = (y[:, 0:A] if a == 0 else merged[:, :]).rearrange("p (g h e) -> p g h e", h=2, e=64)
                        dve.tensor_tensor(out, pairs[:, a, :, 0:P].rearrange("p g (h e) -> p g h e", e=64),
                                          lift[:, a, :].rearrange("p (g h e) -> p g h e", h=2, e=1).to_broadcast([P, attn_heads // 2, 2, 64]), ALU.mult)
                        dve.drain()
                        if a:
                            dve.tensor_tensor(y[:, 0:A], y[:, 0:A], merged[:, :], ALU.add)
                            dve.drain()
                dve.wait_ge(squared, n + 1)
                dve.tensor_scalar(rstd[:, :], ss[:, :], 1.0 / V, EPS1, ALU.mult, ALU.add).then_inc(var_done, 1)
                dve.wait_ge(std_done, n + 1)
                dve.reciprocal(rstd[:, :], std[:, :])
                dve.drain()
                for h in range(H):
                    c = slice(h * V, (h + 1) * V)
                    last = dve.scalar_tensor_tensor(out=y[:, A + h * V:A + (h + 1) * V], in0=of[:, b, c], scalar=rstd[:, h:h + 1],
                                                    in1=gains[:, c], op0=ALU.mult, op1=ALU.mult)
                last.then_inc(normed, 1)

            def slot(i, b, first, last):
                n = 2 * i + b
                if not last:
                    front(*after(i, b))
                dve.drain()
                dve.wait_ge(x_loaded[b], 16 * i + 16)
                dve.wait_ge(z_made, n + 1)
                wait(dve, x_done, n)
                for h in range(2):
                    c = slice(h * BANK, (h + 1) * BANK)
                    moved = dve.scalar_tensor_tensor(out=z[:, c], in0=xt[:, b, c], scalar=alpha, in1=ps_z[h][:, :],
                                                     op0=ALU.mult, op1=ALU.add)
                moved.then_inc(z_moved, 1)
                dve.drain()
                for h in range(2):
                    dve.bn_stats(bn[:, h, :], z[:, h * BANK:(h + 1) * BANK])
                dve.drain()
                dve.bn_aggr(mv[:, :], bn[:, :, :]).then_inc(lvar_done, 1)
                dve.wait_ge(lstd_done, n + 1)
                dve.reciprocal(lrstd[:, :], lstd[:, :])
                dve.drain()
                dve.tensor_scalar(z[:, :], z[:, :], mv[:, 0:1], lrstd[:, 0:1], ALU.subtract, ALU.mult).then_inc(centred, 1)

            dve.wait_ge(vec_loaded, 48)
            front(0, 0)
            tiles(dve, slot)


AH, AE = 8, 64
DILATIONS = (1, 4, 16)
REL_BUCKETS, REL_MAX = 32, 1024
STEP = AE
VEC = 384
VPAD = 256
PAIR = P + 4
NEG = -1e30
TABLES = ((0, 0, 256), (0, 64, 256), (0, 0, 192), (1, 64, 256), (1, 0, 192), (2, 0, 128))
TAB_AT = (0, 256, 512, 768, 1024, 1280)
TAB_WIDTH = (256, 256, 256, 256, 256, 128)
TAB_W = 1408


def bucket_constant():
    half = REL_BUCKETS // 2
    exact = half // 2
    out = np.zeros((REL_BUCKETS + 1, len(DILATIONS), VEC), np.float32)
    for n, dil in enumerate(DILATIONS):
        off = np.arange(VEC) - (P - 1) - STEP
        inside = np.abs(off) <= STEP
        if n == 2:
            inside = (np.arange(VEC) - (P - 1)) % 2 == 0
            off = (np.arange(VEC) - (P - 1)) // 2
            inside &= np.abs(off) <= STEP
        rel = off * dil
        dist = np.abs(rel)
        large = exact + (np.log(np.maximum(dist, 1) / exact) / np.log(REL_MAX / exact) * (half - exact)).astype(np.int32)
        bucket = np.where(rel > 0, half, 0) + np.where(dist < exact, dist, np.minimum(large, half - 1))
        out[bucket[inside], n, np.nonzero(inside)[0]] = 1.0
        out[REL_BUCKETS, n, ~inside] = NEG
    return out[:, :, ::-1]


def bias_vectors(nc, tag, rel_bias, buckets, vectors, vpad):
    with ExitStack() as ctx:
        sb = lambda n, s, d=F32: ctx.enter_context(nc.sbuf_tensor(f"{tag}_{n}", s, d))
        sem = own_semaphores(nc, ctx, tag)
        rb, bk = sb("rb", [REL_BUCKETS + 1, AH]), sb("bk", [REL_BUCKETS + 1, 3 * VEC])
        zero = sb("zero", [P, AH * AE])
        vec = sb("vec", [AH, 3 * VEC])
        ps = [ctx.enter_context(nc.psum_tensor(f"{tag}_ps{n}", [P, BANK], F32)) for n in range(3)]
        loaded, set_, made, moved, zeroed, stored = sem("loaded"), sem("set"), sem("made"), sem("moved"), sem("zeroed"), sem("stored")
        block = ctx.enter_context(nc.Block())

        @block.sync
        def _(sp):
            sp.dma_start(rb[0:REL_BUCKETS, :], rel_bias).then_inc(loaded, 16)
            sp.dma_start(bk[:, :], buckets).then_inc(loaded, 16)
            sp.wait_ge(zeroed, 2)
            for first in (0, VPAD, VPAD + SEQ, VPAD + SEQ + P):
                if first != VPAD:
                    sp.dma_start(vpad[first:first + P, :], zero[:, :]).then_inc(stored, 16)
            sp.dma_start(vpad[P:2 * P, :], zero[:, :]).then_inc(stored, 16)
            sp.wait_ge(moved, 3)
            sp.dma_start(vectors, vec[:, :]).then_inc(stored, 16)
            sp.wait_ge(stored, 80)

        @block.vector
        def _(dve):
            dve.memset(zero[:, :], 0.0).then_inc(zeroed, 1)
            dve.memset(rb[REL_BUCKETS:REL_BUCKETS + 1, :], 1.0).then_inc(zeroed, 1)
            for n in range(3):
                dve.wait_ge(made, n + 1)
                dve.tensor_scalar(vec[:, n * VEC:(n + 1) * VEC], ps[n][0:AH, 0:VEC], 8.0, None, ALU.mult).then_inc(moved, 1)

        @block.tensor
        def _(pe):
            pe.wait_ge(loaded, 32)
            pe.wait_ge(zeroed, 2)
            for n in range(3):
                pe.matmul(ps[n][0:AH, 0:VEC], rb[:, :], bk[:, n * VEC:(n + 1) * VEC], start=True, stop=True).then_inc(made, 1)


def dilated_attention(nc, tag, qT, kT, vpad, vectors, attn):
    ST = 3 * TILES
    KP = VPAD + SEQ + VPAD
    with ExitStack() as ctx:
        sb = lambda n, s, d=F32: ctx.enter_context(nc.sbuf_tensor(f"{tag}_{n}", s, d))
        sem = own_semaphores(nc, ctx, tag)
        pbank = lambda n: ctx.enter_context(nc.psum_tensor(f"{tag}_{n}", [P, BANK], F32))
        q = sb("q", [P, 2, SEQ])
        k = sb("k", [P, 2, KP])
        v = sb("v", [P, 2, 9 + 12 + 8, P])
        tab = sb("tab", [P, 2, 2, TAB_W])
        ident = sb("ident", [P, P])
        s_sb = sb("s_sb", [P, 2, 2, 256])
        p_sb = sb("p_sb", [P, 2, 2, 256])
        pT = sb("pT", [P, 2, 2, 2, P])
        shift = sb("shift", [P, 2, 2])
        stage = sb("stage", [P, ST, PAIR])
        ps_s = [[pbank(f"ps_s{a}{h}") for h in range(2)] for a in range(2)]
        ps_t = [pbank(f"ps_t{h}") for h in range(2)]
        ps_o = [pbank(f"ps_o{h}") for h in range(2)]
        LOADS = 2 + 6 + 12
        STORES = (1, 4, 1)
        loaded = [sem("loaded0"), sem("loaded1")]
        consts, scored, biased, p_done, p_turned = sem("consts"), sem("scored"), sem("biased"), sem("p_done"), sem("p_turned")
        moved = [sem("p_moved_act"), sem("p_moved_dve")]
        o_made = sem("o_made")
        o_moved = [sem("o_moved_act"), sem("o_moved_dve")]
        stored = [sem(f"stored{n}") for n in range(3)]
        block = ctx.enter_context(nc.Block())

        def pairs(eng, pair):
            for n in range(AH // 2):
                pair(0, n)

        def step_at(i, j, more):
            return 2 * ST * i + (ST * j + more)

        def table_of(d, t):
            if d == 0:
                return 1 if t == 0 else 2 if t == TILES - 1 else 0
            return 3 + t % 2 if d == 1 else 5

        def wide(d):
            return P if d == 2 else 2 * P

        def queries(tile, d, t, rows):
            if d == 0:
                return tile[rows, t * P:(t + 1) * P]
            if d == 1:
                first = t // 2 + 4 * P * (t % 2)
                return tile[rows, first:first + 4 * (P - 1) + 1:4]
            return tile[rows, t:SEQ:TILES]

        def keys(tile, d, t, rows):
            if d == 0:
                return tile[rows, VPAD - STEP + t * P:VPAD - STEP + t * P + 256]
            if d == 1:
                first = VPAD + t // 2 + 4 * (P * (t % 2) - STEP)
                return tile[rows, first:first + 4 * 255 + 1:4]
            return tile[rows, VPAD + t:VPAD + SEQ:TILES]

        def v_block(d, t):
            return t if d == 0 else 9 + 3 * (t // 2) + t % 2 if d == 1 else 21 + t

        @block.sync
        def _(sp):
            def load(i, j, b):
                rows = bass.ds(2 * P * i + P * j, P)
                sp.dma_start(q[:, b, :], qT[rows, :]).then_inc(loaded[b], 16)
                sp.dma_start(k[:, b, VPAD:VPAD + SEQ], kT[rows, :]).then_inc(loaded[b], 16)
                sp.dma_start(v[:, b, 0:9, :], vpad[VPAD - STEP:VPAD - STEP + 9 * P, rows].rearrange("(j p) c -> p j c", p=P)).then_inc(loaded[b], 16)
                for r in range(4):
                    sp.dma_start(v[:, b, 9 + 3 * r:12 + 3 * r, :],
                                 vpad[:, rows].rearrange("(j p r) c -> r p j c", p=P, r=4)[r]).then_inc(loaded[b], 16)
                sp.dma_start(v[:, b, 21:29, :], vpad[VPAD:VPAD + SEQ, rows].rearrange("(p t) c -> p t c", t=TILES)).then_inc(loaded[b], 16)
                for h in range(2):
                    head = vectors[4 * i + 2 * j + h:4 * i + 2 * j + h + 1, :]
                    for n, (d, c0, c1) in enumerate(TABLES):
                        at = TAB_AT[n] + TAB_WIDTH[n]
                        src = bass.AP(head.tensor, head.offset + d * VEC + VEC - P + 1 - c1, [[1, P], [1, c1 - c0]])
                        sp.dma_start(tab[:, b, h, at - c1:at - c0], src).then_inc(loaded[b], 16)

            def store(i, j):
                cols = bass.ds(2 * PAIR * i + PAIR * j, PAIR)
                for d in range(3):
                    for h in range(2):
                        sp.wait_ge(o_moved[h], step_at(i, j, TILES * (d + 1)))
                    mine = stage[:, TILES * d:TILES * (d + 1), :]
                    if d == 0:
                        sp.dma_start(attn[d, :, cols].rearrange("(t p) c -> p t c", p=P), mine).then_inc(stored[d], 16)
                    elif d == 1:
                        for r in range(4):
                            sp.dma_start(attn[d, :, cols].rearrange("(h p r) c -> r p h c", p=P, r=4)[r],
                                         mine[:, 2 * r:2 * r + 2, :]).then_inc(stored[d], 16)
                    else:
                        sp.dma_start(attn[d, :, cols].rearrange("(p t) c -> p t c", t=TILES), mine).then_inc(stored[d], 16)

            sp.wait_ge(consts, 1)
            load(0, 0, 0)
            load(0, 1, 1)

            for n in range(AH // 2):
                store(0, n)
                if n + 2 < AH // 2:
                    sp.wait_ge(o_made, step_at(0, n, ST))
                    load(0, n + 2, n % 2)
            for d in range(3):
                sp.wait_ge(stored[d], 16 * STORES[d] * AH // 2)

        @block.gpsimd
        def _(pool):
            make_identity(pool, ident)
            for b in range(2):
                pool.memset(k[:, b, 0:VPAD], 0.0)
                pool.memset(k[:, b, VPAD + SEQ:KP], 0.0)
                pool.memset(tab[:, b, :, :], 8 * NEG)
            pool.drain()
            pool.memset(ident[0:1, 0:1], 1.0).then_inc(consts, 1)

        @block.tensor
        def _(pe):
            pe.wait_ge(consts, 1)

            def score(i, j, s):
                b = j % 2
                d, t = s // TILES, s % TILES
                wait(pe, biased, step_at(i, j, s - 1))
                for h in range(2):
                    rows = slice(h * AE, (h + 1) * AE)
                    last = pe.matmul(ps_s[s % 2][h][:, 0:wide(d)], queries(q[:, b, :], d, t, rows), keys(k[:, b, :], d, t, rows),
                                     start=True, stop=True)
                last.then_inc(scored, 1)

            def turn(i, j, s):
                d = s // TILES
                pe.wait_ge(p_done, step_at(i, j, s + 1))
                for h in range(2):
                    wait(pe, moved[h], step_at(i, j, s))
                    for c in range(wide(d) // P):
                        last = pe.transpose(ps_t[h][:, c * P:(c + 1) * P], p_sb[:, s % 2, h, c * P:(c + 1) * P], ident[:, :])
                last.then_inc(p_turned, 1)

            def values(i, j, s):
                b = j % 2
                d, t = s // TILES, s % TILES
                for h in range(2):
                    pe.wait_ge(moved[h], step_at(i, j, s + 1))
                    wait(pe, o_moved[h], step_at(i, j, s))
                    n = wide(d) // P
                    for c in range(n):
                        last = pe.matmul(ps_o[h][:, 0:AE], pT[:, s % 2, h, c, :], v[:, b, v_block(d, t) + c, h * AE:(h + 1) * AE],
                                         start=(c == 0), stop=(c == n - 1))
                last.then_inc(o_made, 1)

            def pair(i, j):
                pe.wait_ge(loaded[j % 2], 16 * LOADS * i + 16 * LOADS * (j // 2 + 1))
                score(i, j, 0)
                score(i, j, 1)
                for s in range(ST):
                    if s < ST - 2:
                        score(i, j, s + 2)
                    turn(i, j, s)
                    if s:
                        values(i, j, s - 1)
                values(i, j, ST - 1)
            pairs(pe, pair)

        @block.vector
        def _(dve):
            dve.wait_ge(consts, 1)

            def bias(i, j, s):
                b = j % 2
                d, t = s // TILES, s % TILES
                dve.wait_ge(scored, step_at(i, j, s + 1))
                wait(dve, p_done, step_at(i, j, s - 1))
                at = TAB_AT[table_of(d, t)]
                for h in range(2):
                    dve.tensor_tensor_reduce(s_sb[:, s % 2, h, 0:wide(d)], ps_s[s % 2][h][:, 0:wide(d)],
                                             tab[:, b, h, at:at + wide(d)][:, ::-1], 1.0, -3e38, ALU.add, ALU.max,
                                             stage[:, s, P + h:P + h + 1])
                dve.drain()
                dve.tensor_scalar(shift[:, s % 2, :], stage[:, s, P:P + 2], -0.125, None, ALU.mult).then_inc(biased, 1)

            def move(i, j, s):
                d = s // TILES
                dve.wait_ge(p_turned, step_at(i, j, s + 1))
                wait(dve, o_made, step_at(i, j, s - 1))
                dve.tensor_copy(pT[:, s % 2, 1, 0:wide(d) // P, :], ps_t[1][:, 0:wide(d)].rearrange("p (c q) -> p c q", q=P)).then_inc(moved[1], 1)

            def move_out(i, j, s):
                dve.wait_ge(o_made, step_at(i, j, s + 1))
                dve.tensor_copy(stage[:, s, AE:2 * AE], ps_o[1][:, 0:AE]).then_inc(o_moved[1], 1)

            def pair(i, j):
                dve.wait_ge(loaded[j % 2], 16 * LOADS * i + 16 * LOADS * (j // 2 + 1))
                for s in range(ST):
                    if s % TILES == 0:
                        d = s // TILES
                        wait(dve, stored[d], 32 * STORES[d] * i + 16 * STORES[d] * j)
                    bias(i, j, s)
                    if s:
                        move(i, j, s - 1)
                    if s > 1:
                        move_out(i, j, s - 2)
                move(i, j, ST - 1)
                move_out(i, j, ST - 2)
                move_out(i, j, ST - 1)
            pairs(dve, pair)

        @block.scalar
        def _(act):
            def exps(i, j, s):
                d = s // TILES
                act.wait_ge(biased, step_at(i, j, s + 1))
                wait(act, p_turned, step_at(i, j, s - 1))
                for h in range(2):
                    last = act.activation(p_sb[:, s % 2, h, 0:wide(d)], s_sb[:, s % 2, h, 0:wide(d)], ACT.Exp,
                                          bias=shift[:, s % 2, h:h + 1], scale=0.125, accum_out=stage[:, s, P + 2 + h:P + 3 + h])
                last.then_inc(p_done, 1)

            def move(i, j, s):
                d = s // TILES
                act.wait_ge(p_turned, step_at(i, j, s + 1))
                wait(act, o_made, step_at(i, j, s - 1))
                act.activation(pT[:, s % 2, 0, 0:wide(d) // P, :], ps_t[0][:, 0:wide(d)].rearrange("p (c q) -> p c q", q=P), ACT.Copy).then_inc(moved[0], 1)

            def move_out(i, j, s):
                act.wait_ge(o_made, step_at(i, j, s + 1))
                act.activation(stage[:, s, 0:AE], ps_o[0][:, 0:AE], ACT.Copy).then_inc(o_moved[0], 1)

            def pair(i, j):
                for s in range(ST):
                    exps(i, j, s)
                    if s:
                        move(i, j, s - 1)
                    if s > 1:
                        move_out(i, j, s - 2)
                move(i, j, ST - 1)
                move_out(i, j, ST - 2)
                move_out(i, j, ST - 1)
            pairs(act, pair)


EPS2 = 1e-6
CTX = 256
ROWS2 = SEQ + CTX
GRID_W = 64
GRID_H = SEQ // GRID_W
RANK = 16


def low_rank_gates(nc, tag, lowT, up, bias, gT):
    C = gT[0].shape[0]
    NT = C // P
    with ExitStack() as ctx:
        sb = lambda n, s, d=F32: ctx.enter_context(nc.sbuf_tensor(f"{tag}_{n}", s, d))
        sem = own_semaphores(nc, ctx, tag)
        low, ups = sb("low", [RANK, 2, SEQ]), sb("ups", [RANK, 2, C])
        shift = sb("shift", [P, 2, NT])
        z, mag, logs, g = sb("z", [P, 2, SEQ]), sb("mag", [P, SEQ]), sb("logs", [P, 2, SEQ]), sb("g", [P, 2, SEQ])
        ps = [[ctx.enter_context(nc.psum_tensor(f"{tag}_ps{a}{h}", [P, BANK], F32)) for h in range(2)] for a in range(2)]
        loaded, made, z_done, ln_done, g_done = sem("loaded"), sem("made"), sem("z_done"), sem("ln_done"), sem("g_done")
        stored = [sem("stored0"), sem("stored1")]
        block = ctx.enter_context(nc.Block())
        units = [(d, c) for d in range(2) for c in range(NT)]

        @block.sync
        def _(sp):
            for d in range(2):
                sp.dma_start(low[:, d, :], lowT[d * RANK:(d + 1) * RANK, :]).then_inc(loaded, 16)
                sp.dma_start(ups[:, d, :], up[d]).then_inc(loaded, 16)
                with nc.allow_non_contiguous_dma(reason="a bias for each partition"):
                    sp.dma_start(shift[:, d, :], bias[d].rearrange("(c p) -> p c", p=P)).then_inc(loaded, 16)
            for n, (d, c) in enumerate(units):
                sp.wait_ge(g_done, n + 1)
                sp.dma_start(gT[d][c * P:(c + 1) * P, :], g[:, n % 2, :]).then_inc(stored[n % 2], 16)
            for b in range(2):
                sp.wait_ge(stored[b], 16 * NT)

        @block.tensor
        def _(pe):
            pe.wait_ge(loaded, 96)
            for n, (d, c) in enumerate(units):
                wait(pe, z_done, 2 * (n - 1))
                for h in range(2):
                    pe.matmul(ps[n % 2][h][:, :], ups[:, d, c * P:(c + 1) * P], low[:, d, h * BANK:(h + 1) * BANK],
                              start=True, stop=True).then_inc(made, 1)

        @block.scalar
        def _(act):
            for n, (d, c) in enumerate(units):
                wait(act, g_done, n - 1)
                for h in range(2):
                    act.wait_ge(made, 2 * n + h + 1)
                    act.activation(z[:, n % 2, h * BANK:(h + 1) * BANK], ps[n % 2][h][:, :], ACT.Identity,
                                   bias=shift[:, d, c:c + 1]).then_inc(z_done, 1)
                act.drain()
                act.activation(mag[:, :], z[:, n % 2, :], ACT.Abs)
                act.drain()
                act.activation(mag[:, :], mag[:, :], ACT.Exp, scale=-1.0)
                act.drain()
                act.activation(logs[:, n % 2, :], mag[:, :], ACT.Ln, bias=1.0).then_inc(ln_done, 1)

        @block.vector
        def _(dve):
            for n in range(len(units)):
                dve.wait_ge(ln_done, n + 1)
                wait(dve, stored[n % 2], 16 * (n // 2))
                dve.scalar_tensor_tensor(out=g[:, n % 2, :], in0=z[:, n % 2, :], scalar=0.0, in1=logs[:, n % 2, :],
                                         op0=ALU.min, op1=ALU.subtract).then_inc(g_done, 1)


def condition(nc, tag, c, c_ctx, sT):
    with ExitStack() as ctx:
        raw = ctx.enter_context(nc.sbuf_tensor(f"{tag}_raw", [P, 2, KB], F32))
        loaded = own_semaphores(nc, ctx, tag)("loaded")
        block = ctx.enter_context(nc.Block())

        @block.sync
        def _(sp):
            with nc.allow_non_contiguous_dma(reason="a vector goes down the partitions"):
                sp.dma_start(raw[:, 0, :], c[0].rearrange("(k p) -> p k", p=P)).then_inc(loaded, 16)
                sp.dma_start(raw[:, 1, :], c_ctx.rearrange("(k p) -> p k", p=P)).then_inc(loaded, 16)

        @block.scalar
        def _(act):
            act.wait_ge(loaded, 32)
            act.activation(sT[:, :, :], raw[:, :, :].rearrange("p r k -> p k r"), ACT.Silu)


def modulate(nc, tag, x, tokens, gain, ada, ada_bias, row, shift_at, scale_at, hT, hT_cols=None, h=None):
    T = tokens // P
    DEPTH = 4
    with ExitStack() as ctx:
        sb = lambda n, s, d=F32: ctx.enter_context(nc.sbuf_tensor(f"{tag}_{n}", s, d))
        sem = own_semaphores(nc, ctx, tag)
        ident = sb("ident", [P, P])
        vecs = sb("vecs", [P, 5, D])
        xt = sb("xt", [P, DEPTH, D])
        squares = sb("squares", [P, D])
        ss, std, rstd = sb("ss", [P, 1]), sb("std", [P, 1]), sb("rstd", [P, 1])
        eps = sb("eps", [P, 1])
        scaled, out = sb("scaled", [P, D]), sb("out", [P, 2, D])
        ps = [ctx.enter_context(nc.psum_tensor(f"{tag}_ps{n}", [P, BANK], F32)) for n in range(4)]
        vec_loaded, consts = sem("vec_loaded"), sem("consts")
        loaded = [sem(f"loaded{b}") for b in range(DEPTH)]
        stored = [sem("stored0"), sem("stored1")]
        ready, squared, std_done, scaled_done, h_done = sem("ready"), sem("squared"), sem("std_done"), sem("scaled_done"), sem("h_done")
        turned, moved = sem("turned"), sem("moved")
        block = ctx.enter_context(nc.Block())

        @block.sync
        def _(sp):
            def load(t):
                if t < T:
                    wait(sp, scaled_done, t - DEPTH + 1)
                    sp.dma_start(xt[:, t % DEPTH, :], x[t * P:(t + 1) * P, :]).then_inc(loaded[t % DEPTH], 16)

            for t in range(DEPTH - 1):
                load(t)
            for n, src in enumerate((gain, ada[row, scale_at:scale_at + D], ada_bias[scale_at:scale_at + D],
                                     ada[row, shift_at:shift_at + D], ada_bias[shift_at:shift_at + D])):
                sp.dma_start(vecs[:, n, :], row_to_all(src, D)).then_inc(vec_loaded, 16)
            for t in range(T):
                load(t + DEPTH - 1)
                if h is not None and t:
                    sp.wait_ge(h_done, t)
                    sp.dma_start(h[(t - 1) * P:t * P, :], out[:, (t - 1) % 2, :]).then_inc(stored[(t - 1) % 2], 16)
            if h is not None:
                sp.wait_ge(h_done, T)
                sp.dma_start(h[(T - 1) * P:T * P, :], out[:, (T - 1) % 2, :]).then_inc(stored[(T - 1) % 2], 16)
                sp.wait_ge(stored[0], 8 * T)
                sp.wait_ge(stored[1], 8 * T)

        def by_columns(pool, t):
            pool.wait_ge(moved, 2 * t + 2)
            for k in range(KB):
                dst = hT_cols[:, k, :].rearrange("p (w r) -> p r w", r=GRID_H)[:, 2 * t:2 * t + 2, :]
                pool.tensor_copy(dst, hT[:, k, t * P:(t + 1) * P].rearrange("p (r w) -> p r w", w=GRID_W))

        @block.gpsimd
        def _(pool):
            make_identity(pool, ident)
            pool.memset(eps[:, :], EPS2)
            pool.drain()
            pool.memset(ident[0:1, 0:1], 1.0).then_inc(consts, 1)
            for t in range(T):
                pool.wait_ge(scaled_done, t + 1)
                wait(pool, turned, 2 * (t - 1))
                if h is not None:
                    wait(pool, stored[t % 2], 16 * (t // 2))
                pool.tensor_tensor(out[:, t % 2, :], scaled[:, :], vecs[:, 3, :], ALU.add).then_inc(h_done, 1)
                if hT_cols is not None and t:
                    by_columns(pool, t - 1)
            if hT_cols is not None:
                by_columns(pool, T - 1)

        @block.vector
        def _(dve):
            dve.wait_ge(vec_loaded, 80)
            dve.scalar_tensor_tensor(out=vecs[:, 1, :], in0=vecs[:, 1, :], scalar=1.0, in1=vecs[:, 2, :], op0=ALU.add, op1=ALU.add)
            dve.tensor_tensor(vecs[:, 3, :], vecs[:, 3, :], vecs[:, 4, :], ALU.add)
            dve.drain()
            dve.tensor_tensor(vecs[:, 0, :], vecs[:, 0, :], vecs[:, 1, :], ALU.mult)
            for t in range(T):
                dve.wait_ge(std_done, t + 1)
                dve.reciprocal(rstd[:, :], std[:, :])
                dve.drain()
                wait(dve, h_done, t)
                dve.scalar_tensor_tensor(out=scaled[:, :], in0=xt[:, t % DEPTH, :], scalar=rstd[:, 0:1], in1=vecs[:, 0, :],
                                         op0=ALU.mult, op1=ALU.mult).then_inc(scaled_done, 1)

        @block.scalar
        def _(act):
            act.wait_ge(consts, 1)

            def norm(t):
                act.drain()
                act.wait_ge(loaded[t % DEPTH], 16 * (t // DEPTH + 1))
                act.activation(squares[:, :], xt[:, t % DEPTH, :], ACT.Square, accum_out=ss[:, :])
                act.drain()
                wait(act, scaled_done, t)
                act.activation(std[:, :], ss[:, :], ACT.Sqrt, scale=1.0 / D, bias=eps[:, 0:1]).then_inc(std_done, 1)

            norm(0)
            for t in range(T):
                if t + 1 < T:
                    norm(t + 1)
                for g in range(2):
                    act.wait_ge(turned, 2 * t + g + 1)
                    act.activation(hT[:, 4 * g:4 * g + 4, t * P:(t + 1) * P],
                                   ps[(2 * t + g) % 4][:, :].rearrange("p (j c) -> p j c", j=4), ACT.Copy).then_inc(moved, 1)

        @block.tensor
        def _(pe):
            pe.wait_ge(consts, 1)
            for t in range(T):
                pe.wait_ge(h_done, t + 1)
                for g in range(2):
                    n = 2 * t + g
                    wait(pe, moved, n - 3)
                    for j in range(4):
                        k = 4 * g + j
                        last = pe.transpose(ps[n % 4][:, j * P:(j + 1) * P], out[:, t % 2, k * P:(k + 1) * P], ident[:, :])
                    last.then_inc(turned, 1)


POOL_WINDOWS = (2, 4, 8, 16)
EDGE = 8


def pool_branch(nc, tag, uT, pool_w, pool_scale, yT):
    G = 64
    WIDE = SEQ + 2 * EDGE
    with ExitStack() as ctx:
        sb = lambda n, s, d=F32: ctx.enter_context(nc.sbuf_tensor(f"{tag}_{n}", s, d))
        sem = own_semaphores(nc, ctx, tag)
        u = sb("u", [P, 3, WIDE])
        s2, s4, s8, s16 = (sb(f"s{n}", [P, 3, WIDE]) for n in POOL_WINDOWS)
        inv = sb("inv", [P, 2, SEQ])
        wt = sb("wt", [P, 2, G])
        scale = sb("scale", [P, 2])
        diff = sb("diff", [P, 2, SEQ])
        y = sb("y", [P, 2, SEQ])
        ps = [[ctx.enter_context(nc.psum_tensor(f"{tag}_ps{g}{h}", [P, BANK], F32)) for h in range(2)] for g in range(4)]
        loaded, padded, diff_done, made, y_done, stored = sem("loaded"), sem("padded"), sem("diff_done"), sem("made"), sem("y_done"), sem("stored")
        block = ctx.enter_context(nc.Block())

        @block.sync
        def _(sp):
            sp.wait_ge(padded, 1)
            sp.dma_start(u[:, 0:2, EDGE:EDGE + SEQ], uT.rearrange("(b p) t -> p b t", p=P)).then_inc(loaded, 16)
            sp.dma_start(wt[:, :, :], pool_w.rearrange("(b g) c d -> (g c) b d", g=2)).then_inc(loaded, 16)
            with nc.allow_non_contiguous_dma(reason="a scale for each partition"):
                sp.dma_start(scale[:, :], pool_scale.rearrange("(b p) -> p b", p=P)).then_inc(loaded, 16)
            sp.wait_ge(y_done, 8)
            sp.dma_start(yT.rearrange("(b p) t -> p b t", p=P), y[:, :, :]).then_inc(stored, 16)
            sp.wait_ge(stored, 16)

        @block.vector
        def _(dve):
            dve.memset(u[:, :, :], 0.0)
            dve.drain()
            dve.memset(u[:, 2, EDGE:EDGE + SEQ], 1.0)
            dve.drain()
            dve.memset(s2[:, :, 0:1], 0.0).then_inc(padded, 1)
            dve.wait_ge(loaded, 48)
            level = u
            for n, s in enumerate((s2, s4, s8, s16)):
                back, ahead = (1, 0) if n == 0 else (1 << (n - 1), 1 << (n - 1))
                lo, hi = (1 << n), WIDE - (1 << n)
                dve.memset(s[:, :, 0:lo], 0.0)
                dve.memset(s[:, :, hi:WIDE], 0.0)
                dve.tensor_tensor(s[:, :, lo:hi], level[:, :, lo - back:hi - back], level[:, :, lo + ahead:hi + ahead], ALU.add)
                dve.drain()
                level = s
            mid = slice(EDGE, EDGE + SEQ)
            for g, s in enumerate((s2, s4, s8, s16)):
                rows = slice(G * (g % 2), G * (g % 2) + G)
                dve.reciprocal(inv[rows, g // 2, :], s[rows, 2, mid])
                dve.drain()
                dve.tensor_tensor(diff[rows, g // 2, :], s[rows, g // 2, mid], inv[rows, g // 2, :], ALU.mult)
                dve.drain()
                dve.tensor_tensor(diff[rows, g // 2, :], diff[rows, g // 2, :], u[rows, g // 2, mid], ALU.subtract).then_inc(diff_done, 1)

        @block.tensor
        def _(pe):
            for g in range(4):
                pe.wait_ge(diff_done, g + 1)
                rows = slice(G * (g % 2), G * (g % 2) + G)
                for h in range(2):
                    pe.matmul(ps[g][h][rows, :], wt[rows, g // 2, :], diff[rows, g // 2, h * BANK:(h + 1) * BANK],
                              start=True, stop=True).then_inc(made, 1)

        @block.scalar
        def _(act):
            for g in range(4):
                rows = slice(G * (g % 2), G * (g % 2) + G)
                for h in range(2):
                    act.wait_ge(made, 2 * g + h + 1)
                    act.activation(y[rows, g // 2, h * BANK:(h + 1) * BANK], ps[g][h][rows, :], ACT.Copy,
                                   scale=scale[rows, g // 2:g // 2 + 1]).then_inc(y_done, 1)


TAPS = 5
T2 = ROWS2 // P
HALO = TAPS // 2
CTX_AT = HALO + SEQ + 2 * HALO
CONV_W = CTX_AT + CTX + HALO


def conv_silu(nc, tag, uT, w, bias, tok, chan=None, chan_from=0):
    C = uT.shape[0]
    NT = C // P
    with ExitStack() as ctx:
        sb = lambda n, s, d=F32: ctx.enter_context(nc.sbuf_tensor(f"{tag}_{n}", s, d))
        sem = own_semaphores(nc, ctx, tag)
        u = sb("u", [P, 2, CONV_W])
        taps, shift = sb("taps", [P, TAPS, NT]), sb("shift", [P, NT])
        acc, out, stage = sb("acc", [P, 2, CONV_W]), sb("out", [P, 2, CONV_W]), sb("stage", [P, 2, T2, P])
        ident = sb("ident", [P, P])
        ps = [[ctx.enter_context(nc.psum_tensor(f"{tag}_ps{a}{g}", [P, BANK], F32)) for g in range(3)] for a in range(2)]
        w_loaded, padded, consts = sem("w_loaded"), sem("padded"), sem("consts")
        loaded = [sem("loaded0"), sem("loaded1")]
        stored = [sem("stored0"), sem("stored1")]
        kept = [sem("kept0"), sem("kept1")]
        conv_done, out_done, turned, moved = sem("conv_done"), sem("out_done"), sem("turned"), sem("moved")
        block = ctx.enter_context(nc.Block())
        GROUPS = ((0, 4), (4, 8), (8, 10))

        def first(t):
            return HALO + t * P if t < TILES else CTX_AT + (t - TILES) * P

        @block.sync
        def _(sp):
            with nc.allow_non_contiguous_dma(reason="taps and biases for each partition"):
                for j in range(TAPS):
                    sp.dma_start(taps[:, j, :], w[j].rearrange("(n p) -> p n", p=P)).then_inc(w_loaded, 16)
                if bias is not None:
                    sp.dma_start(shift[:, :], bias.rearrange("(n p) -> p n", p=P)).then_inc(w_loaded, 16)
            sp.wait_ge(padded, 1)

            def load(n):
                wait(sp, conv_done, n - 1)
                sp.dma_start(u[:, n % 2, HALO:HALO + SEQ], uT[n * P:(n + 1) * P, 0:SEQ]).then_inc(loaded[n % 2], 16)
                sp.dma_start(u[:, n % 2, CTX_AT:CTX_AT + CTX], uT[n * P:(n + 1) * P, SEQ:ROWS2]).then_inc(loaded[n % 2], 16)

            def keep(n):
                sp.wait_ge(out_done, n + 1)
                rows = slice(n * P - chan_from, (n + 1) * P - chan_from)
                sp.dma_start(chan[rows, 0:SEQ], out[:, n % 2, HALO:HALO + SEQ]).then_inc(kept[n % 2], 16)
                sp.dma_start(chan[rows, SEQ:ROWS2], out[:, n % 2, CTX_AT:CTX_AT + CTX]).then_inc(kept[n % 2], 16)

            load(0)
            for n in range(NT):
                if n + 1 < NT:
                    load(n + 1)
                if chan is not None and n * P >= chan_from:
                    keep(n)
            if chan is not None:
                for b in range(2):
                    sp.wait_ge(kept[b], 32 * sum(n * P >= chan_from for n in range(b, NT, 2)))

        @block.gpsimd
        def _(pool):
            pool.memset(u[:, :, :], 0.0)
            make_identity(pool, ident)
            pool.memset(ident[0:1, 0:1], 1.0).then_inc(consts, 1)
            pool.memset(u[:, :, 0:1], 0.0).then_inc(padded, 1)

        @block.vector
        def _(dve):
            dve.wait_ge(w_loaded, 16 * (TAPS + (bias is not None)))
            for n in range(NT):
                dve.wait_ge(loaded[n % 2], 32 * (n // 2 + 1))
                wait(dve, out_done, n - 1)
                m = CONV_W - 2 * HALO
                a = acc[:, n % 2, HALO:HALO + m]
                last = dve.tensor_scalar(a, u[:, n % 2, 0:m], taps[:, 0, n:n + 1], None, ALU.mult)
                for j in range(1, TAPS):
                    dve.drain()
                    last = dve.scalar_tensor_tensor(out=a, in0=u[:, n % 2, j:j + m], scalar=taps[:, j, n:n + 1], in1=a,
                                                    op0=ALU.mult, op1=ALU.add)
                last.then_inc(conv_done, 1)

        @block.scalar
        def _(act):
            def silu(n):
                act.wait_ge(conv_done, n + 1)
                wait(act, turned, 3 * (n - 1))
                if chan is not None and n >= 2 and (n - 2) * P >= chan_from:
                    act.wait_ge(kept[n % 2], 32 * sum(k * P >= chan_from for k in range(n % 2, n, 2)))
                m = slice(HALO, CONV_W - HALO)
                act.activation(out[:, n % 2, m], acc[:, n % 2, m], ACT.Silu,
                               bias=shift[:, n:n + 1] if bias is not None else 0.0).then_inc(out_done, 1)

            silu(0)
            for n in range(NT):
                if n + 1 < NT:
                    silu(n + 1)
                wait(act, stored[n % 2], 16 * (n // 2))
                for g, (a, b) in enumerate(GROUPS):
                    act.wait_ge(turned, 3 * n + g + 1)
                    act.activation(stage[:, n % 2, a:b, :], ps[n % 2][g][:, 0:(b - a) * P].rearrange("p (t c) -> p t c", c=P),
                                   ACT.Copy).then_inc(moved, 1)
                act.wait_ge(moved, 3 * (n + 1))
                act.dma_start(tok[:, n * P:(n + 1) * P].rearrange("(t p) c -> p t c", p=P), stage[:, n % 2, :, :]).then_inc(stored[n % 2], 16)
            act.wait_ge(stored[0], 16 * ((NT + 1) // 2))
            act.wait_ge(stored[1], 16 * (NT // 2))

        @block.tensor
        def _(pe):
            pe.wait_ge(consts, 1)
            for n in range(NT):
                pe.wait_ge(out_done, n + 1)
                for g, (a, b) in enumerate(GROUPS):
                    wait(pe, moved, 3 * (n - 2) + g + 1)
                    for t in range(a, b):
                        last = pe.transpose(ps[n % 2][g][:, (t - a) * P:(t - a + 1) * P], out[:, n % 2, first(t):first(t) + P], ident[:, :])
                    last.then_inc(turned, 1)


SH = 6
SE = 64
SW = SH * SE
N_STATE = 128


def decay_masks(pool, mask, strict=False):
    pool.memset(mask[:, :, :], 1.0)
    pool.drain()
    for d in range(2):
        sign = 1 if d == FWD else -1
        pool.affine_select(out=mask[:, d, :], in_=mask[:, d, :], compare_op=ALU.is_ge, fill=0.0, base=-1 if strict else 0,
                           pattern=[[sign, P]], channel_multiplier=-sign)
    pool.drain()


def token_decays(nc, tag, dt_raw, dt_bias, a_log, ab, gdn_bias, gdn_a_log, dt, beta, cum, from_start, to_end, whole, logs):
    N = 4 * SH
    with ExitStack() as ctx:
        sb = lambda n, s, d=F32: ctx.enter_context(nc.sbuf_tensor(f"{tag}_{n}", s, d))
        sem = own_semaphores(nc, ctx, tag)
        raw, shift, rate = sb("raw", [P, T2, N]), sb("shift", [P, N]), sb("rate", [P, N])
        b_raw = sb("b_raw", [P, T2, 2 * SH])
        mag, soft = sb("mag", [P, T2, N]), sb("soft", [P, T2, N])
        rest = sb("rest", [P, T2, N])
        tri, ones = sb("tri", [P, 2, P]), sb("ones", [P, P])
        ps = [ctx.enter_context(nc.psum_tensor(f"{tag}_ps{n}", [P, BANK], F32)) for n in range(3)]
        loaded, consts, shifted, ln_done, rate_done, logs_done, made, cum_done, rest_done = (
            sem(n) for n in ("loaded", "consts", "shifted", "ln_done", "rate_done", "logs_done", "made", "cum_done", "rest_done"))
        block = ctx.enter_context(nc.Block())

        @block.sync
        def _(sp):
            with nc.allow_non_contiguous_dma(reason="a few columns of each token"):
                sp.dma_start(raw[:, :, 0:2 * SH], dt_raw.rearrange("(t p) c -> p t c", p=P)).then_inc(loaded, 16)
                sp.dma_start(raw[:, :, 2 * SH:N], ab[:, SW:SW + 2 * SH].rearrange("(t p) c -> p t c", p=P)).then_inc(loaded, 16)
                sp.dma_start(b_raw[:, :, :], ab[:, SW + 2 * SH:SW + 4 * SH].rearrange("(t p) c -> p t c", p=P)).then_inc(loaded, 16)
            flat = lambda t: t.rearrange("a b -> (a b)")
            for dst, src in ((shift[:, 0:2 * SH], dt_bias), (shift[:, 2 * SH:N], gdn_bias), (rate[:, 0:2 * SH], a_log), (rate[:, 2 * SH:N], gdn_a_log)):
                sp.dma_start(dst, row_to_all(flat(src), 2 * SH)).then_inc(loaded, 16)

        @block.gpsimd
        def _(pool):
            decay_masks(pool, tri)
            pool.memset(ones[:, :], 1.0).then_inc(consts, 1)

        @block.vector
        def _(dve):
            dve.wait_ge(loaded, 112)
            dve.tensor_tensor(raw[:, :, :], raw[:, :, :], shift[:, :].rearrange("p (a n) -> p a n", a=1).to_broadcast([P, T2, N]), ALU.add)
            dve.drain()
            dve.scalar_tensor_tensor(out=mag[:, :, :], in0=raw[:, :, :], scalar=-1.0, in1=raw[:, :, :], op0=ALU.mult, op1=ALU.max).then_inc(shifted, 1)
            dve.wait_ge(ln_done, 1)
            dve.scalar_tensor_tensor(out=soft[:, :, :], in0=raw[:, :, :], scalar=0.0, in1=mag[:, :, :], op0=ALU.max, op1=ALU.add)
            dve.drain()
            dve.tensor_copy(dt[:, :, :], soft[:, :, 0:2 * SH])
            dve.wait_ge(rate_done, 1)
            dve.scalar_tensor_tensor(out=logs[:, :, :], in0=soft[:, :, :], scalar=-1.0,
                                     in1=rate[:, :].rearrange("p (a n) -> p a n", a=1).to_broadcast([P, T2, N]),
                                     op0=ALU.mult, op1=ALU.mult).then_inc(logs_done, 1)
            dve.wait_ge(made, 1)
            split = lambda t: t.rearrange("p t (m d h) -> p t m d h", m=2, d=2)
            for d in range(2):
                dve.tensor_copy(split(cum[:, :, :])[:, :, :, d], split(ps[d][:, 0:T2 * N].rearrange("p (t n) -> p t n", n=N))[:, :, :, d])
            dve.drain()
            dve.tensor_tensor(rest[:, :, :], ps[2][:, 0:T2 * N].rearrange("p (t n) -> p t n", n=N), cum[:, :, :], ALU.subtract).then_inc(cum_done, 1)

        @block.scalar
        def _(act):
            act.wait_ge(loaded, 112)
            act.activation(beta[:, :, :], b_raw[:, :, :], ACT.Sigmoid)
            act.activation(rate[:, :], rate[:, :], ACT.Exp).then_inc(rate_done, 1)
            act.wait_ge(shifted, 1)
            act.activation(mag[:, :, :], mag[:, :, :], ACT.Exp, scale=-1.0)
            act.drain()
            act.activation(mag[:, :, :], mag[:, :, :], ACT.Ln, bias=1.0).then_inc(ln_done, 1)
            act.wait_ge(cum_done, 1)
            act.activation(from_start[:, :, :], cum[:, :, :], ACT.Exp)
            act.activation(to_end[:, :, :], rest[:, :, :], ACT.Exp)
            act.activation(whole[:, :, :], ps[2][:, 0:T2 * N].rearrange("p (t n) -> p t n", n=N), ACT.Exp)

        @block.tensor
        def _(pe):
            pe.wait_ge(consts, 1)
            pe.wait_ge(logs_done, 1)
            for n, m in enumerate((tri[:, 0, :], tri[:, 1, :], ones[:, :])):
                last = pe.matmul(ps[n][:, 0:T2 * N], m, logs[:, :, :].rearrange("p t n -> p (t n)"), start=True, stop=True)
            last.then_inc(made, 1)


def order(step, d):
    if step < 2:
        return TILES + (step if d == FWD else 1 - step)
    return step - 2 if d == FWD else TILES - 1 - (step - 2)


STEPS = T2
CTX_STEPS = CTX // P
LAT_UNITS = 2 * TILES


def spread(small, heads, width):
    return small.rearrange("p (h e) -> p h e", e=1).to_broadcast([P, heads, width])


def by_head(t, width=SE):
    return t.rearrange("p (h e) -> p h e", e=width)


def ssd_scan(nc, tag, tok, chan, z, d_skip, norm_g, dt, cum, from_start, to_end, whole, logs, y_out):
    BC = 2 * N_STATE
    HG = SH // 2 * SE
    with ExitStack() as ctx:
        sb = lambda n, s, d=F32: ctx.enter_context(nc.sbuf_tensor(f"{tag}_{n}", s, d))
        sem = own_semaphores(nc, ctx, tag)
        pbank = lambda n: ctx.enter_context(nc.psum_tensor(f"{tag}_{n}", [P, BANK], F32))
        xs, b_tok = sb("xs", [P, T2, SW]), sb("b_tok", [P, T2, BC])
        bc_T = sb("bc_T", [P, 4, ROWS2])
        gate = sb("gate", [P, TILES, SW])
        skip, norm = sb("skip", [P, SH]), sb("norm", [P, SW])
        mask = sb("mask", [P, 2, P])
        xdt, xw = sb("xdt", [P, 2, T2, SW]), sb("xw", [P, 2, T2, SW])
        sm = sb("sm", [P, 2, SH, P])
        gm = sb("gm", [P, 2, 2, P])
        inter, both = sb("inter", [P, 2, SW]), sb("both", [P, 2, SW])
        state, kept = sb("state", [P, 2, SW]), sb("kept", [P, SW])
        Y = sb("Y", [P, TILES, SW])
        ss, std = sb("ss", [P, TILES]), sb("std", [P, TILES])
        ps_r = [pbank("ps_r0"), pbank("ps_r1")]
        ps_g, ps_y, ps_i, ps_u = pbank("ps_g"), pbank("ps_y"), pbank("ps_i"), pbank("ps_u")
        loaded, consts, xdt_done, xw_done, y_set = (sem(n) for n in ("loaded", "consts", "xdt_done", "xw_done", "y_set"))
        r_made, g_made, arg_done, gm_done, exp_done, sm_done = (sem(n) for n in ("r_made", "g_made", "arg_done", "gm_done", "exp_done", "sm_done"))
        backed, updated, state_done, both_done, y_added = (sem(n) for n in ("backed", "updated", "state_done", "both_done", "y_added"))
        gate_done, gated, squared, std_done, normed, stored = (sem(n) for n in ("gate_done", "gated", "squared", "std_done", "normed", "stored"))
        block = ctx.enter_context(nc.Block())

        def place(u):
            return order(u // 2, u % 2), u % 2

        @block.sync
        def _(sp):
            rows = lambda a: a.rearrange("(t p) c -> p t c", p=P)
            sp.dma_start(xs[:, :, :], rows(tok[:, 0:SW])).then_inc(loaded, 16)
            sp.dma_start(b_tok[:, :, :], rows(tok[:, SW:SW + BC])).then_inc(loaded, 16)
            sp.dma_start(bc_T[:, :, :], chan.rearrange("(k p) t -> p k t", p=P)).then_inc(loaded, 16)
            sp.dma_start(gate[:, :, :], rows(z)).then_inc(loaded, 16)
            sp.dma_start(skip[:, :], row_to_all(d_skip, SH)).then_inc(loaded, 16)
            sp.dma_start(norm[:, :], row_to_all(norm_g, SW)).then_inc(loaded, 16)
            sp.wait_ge(normed, TILES)
            sp.dma_start(rows(y_out), Y[:, :, :]).then_inc(stored, 16)
            sp.wait_ge(stored, 16)

        @block.gpsimd
        def _(pool):
            decay_masks(pool, mask)
            pool.memset(mask[0:1, 0, 0:1], 1.0).then_inc(consts, 1)
            pool.wait_ge(loaded, 96)
            for d in range(2):
                pool.wait_ge(xdt_done, T2 * (d + 1))
                for t in range(T2):
                    pool.tensor_tensor(by_head(xw[:, d, t, :]), by_head(xdt[:, d, t, :]),
                                       spread(to_end[:, t, d * SH:(d + 1) * SH], SH, SE), ALU.mult).then_inc(xw_done, 1)
            for t in range(TILES):
                pool.tensor_tensor(by_head(Y[:, t, :]), by_head(xs[:, t, :]), spread(skip[:, :], SH, SE), ALU.mult).then_inc(y_set, 1)

            def add(n):
                t, _ = place(n + 2 * CTX_STEPS)
                pool.wait_ge(both_done, n + 1)
                pool.tensor_tensor(Y[:, t, :], Y[:, t, :], both[:, n % 2, :], ALU.add).then_inc(y_added, 1)

            for n in range(LAT_UNITS):
                pool.wait_ge(exp_done, n + 1)
                pool.wait_ge(gm_done, n + 1)
                for g in range(2):
                    part = sm[:, n % 2, 3 * g:3 * g + 3, :]
                    last = pool.tensor_tensor(part, part, gm[:, n % 2, g:g + 1, :].to_broadcast([P, 3, P]), ALU.mult)
                last.then_inc(sm_done, 1)
                if n:
                    pool.drain()
                    add(n - 1)
            pool.drain()
            add(LAT_UNITS - 1)

        @block.tensor
        def _(pe):
            pe.wait_ge(consts, 1)
            pe.wait_ge(loaded, 96)

            def front(n):
                t, d = place(n + 2 * CTX_STEPS)
                wait(pe, arg_done, n)
                for h in range(SH):
                    col = d * SH + h
                    last = pe.matmul(ps_r[h // 3][:, (h % 3) * P:(h % 3 + 1) * P], logs[:, t, col:col + 1].to_broadcast([P, P]),
                                     mask[:, d, :], start=True, stop=True)
                last.then_inc(r_made, 1)
                wait(pe, gm_done, n)
                for g in range(2):
                    cols = slice(t * P, (t + 1) * P)
                    last = pe.matmul(ps_g[:, g * P:(g + 1) * P], bc_T[:, g, cols], bc_T[:, 2 + g, cols], start=True, stop=True)
                last.then_inc(g_made, 1)

            def update(u):
                t, d = place(u)
                pe.wait_ge(xw_done, T2 * d + t + 1)
                wait(pe, state_done, u)
                for g in range(2):
                    last = pe.matmul(ps_u[:, g * HG:(g + 1) * HG], b_tok[:, t, g * N_STATE:(g + 1) * N_STATE],
                                     xw[:, d, t, g * HG:(g + 1) * HG], start=True, stop=True)
                last.then_inc(updated, 1)

            def back(n):
                u = n + 2 * CTX_STEPS
                t, d = place(u)
                pe.wait_ge(sm_done, n + 1)
                pe.wait_ge(both_done, n)
                for h in range(SH):
                    pe.matmul(ps_y[:, h * SE:(h + 1) * SE], sm[:, n % 2, h, :], xdt[:, d, t, h * SE:(h + 1) * SE], start=True, stop=True)
                pe.wait_ge(state_done, u - 1)
                for g in range(2):
                    last = pe.matmul(ps_i[:, g * HG:(g + 1) * HG], bc_T[:, 2 + g, t * P:(t + 1) * P], state[:, d, g * HG:(g + 1) * HG],
                                     start=True, stop=True)
                last.then_inc(backed, 1)
                if n < LAT_UNITS - 2:
                    update(u)

            front(0)
            for u in range(2 * CTX_STEPS):
                update(u)
            for n in range(LAT_UNITS):
                if n + 1 < LAT_UNITS:
                    front(n + 1)
                back(n)

        @block.vector
        def _(dve):
            dve.wait_ge(loaded, 96)
            dve.wait_ge(consts, 1)
            for d in range(2):
                for t in range(T2):
                    dve.tensor_tensor(by_head(xdt[:, d, t, :]), by_head(xs[:, t, :]), spread(dt[:, t, d * SH:(d + 1) * SH], SH, SE),
                                      ALU.mult).then_inc(xdt_done, 1)

            def args(n):
                t, d = place(n + 2 * CTX_STEPS)
                dve.wait_ge(r_made, n + 1)
                wait(dve, backed, n - 1)
                for h in range(SH):
                    col = d * SH + h
                    last = dve.tensor_scalar(sm[:, n % 2, h, :], ps_r[h // 3][:, (h % 3) * P:(h % 3 + 1) * P], cum[:, t, col:col + 1], 0.0,
                                             ALU.subtract, ALU.min)
                last.then_inc(arg_done, 1)
                dve.wait_ge(g_made, n + 1)
                wait(dve, sm_done, n - 1)
                dve.tensor_tensor(gm[:, n % 2, :, :], ps_g[:, 0:2 * P].rearrange("p (g i) -> p g i", g=2),
                                  mask[:, d:d + 1, :].to_broadcast([P, 2, P]), ALU.mult).then_inc(gm_done, 1)

            def take(u):
                t, d = place(u)
                dve.wait_ge(updated, u + 1)
                s = state[:, d, :]
                if u < 2:
                    dve.tensor_copy(s, ps_u[:, 0:SW]).then_inc(state_done, 1)
                    return
                dve.drain()
                dve.tensor_tensor(by_head(kept[:, :]), by_head(s), spread(whole[:, t, d * SH:(d + 1) * SH], SH, SE), ALU.mult)
                dve.drain()
                dve.tensor_tensor(s, ps_u[:, 0:SW], kept[:, :], ALU.add).then_inc(state_done, 1)

            def outs(n):
                u = n + 2 * CTX_STEPS
                t, d = place(u)
                dve.wait_ge(backed, n + 1)
                dve.tensor_tensor(by_head(inter[:, n % 2, :]), by_head(ps_i[:, 0:SW]), spread(from_start[:, t, d * SH:(d + 1) * SH], SH, SE), ALU.mult)
                wait(dve, y_added, n - 1)
                dve.drain()
                dve.tensor_tensor(both[:, n % 2, :], ps_y[:, 0:SW], inter[:, n % 2, :], ALU.add).then_inc(both_done, 1)
                if n < LAT_UNITS - 2:
                    take(u)

            args(0)
            for u in range(2 * CTX_STEPS):
                take(u)
            for n in range(LAT_UNITS):
                if n + 1 < LAT_UNITS:
                    args(n + 1)
                outs(n)
            dve.wait_ge(y_added, LAT_UNITS)
            dve.wait_ge(gate_done, 1)
            for t in range(TILES):
                dve.tensor_tensor(Y[:, t, :], Y[:, t, :], gate[:, t, :], ALU.mult).then_inc(gated, 1)
            dve.wait_ge(squared, TILES)
            dve.tensor_scalar(ss[:, :], ss[:, :], 1.0 / SW, EPS2, ALU.mult, ALU.add).then_inc(squared, 1)
            dve.wait_ge(std_done, 1)
            dve.reciprocal(ss[:, :], std[:, :])
            dve.drain()
            for t in range(TILES):
                dve.scalar_tensor_tensor(out=Y[:, t, :], in0=Y[:, t, :], scalar=ss[:, t:t + 1], in1=norm[:, :],
                                         op0=ALU.mult, op1=ALU.mult).then_inc(normed, 1)

        @block.scalar
        def _(act):
            act.wait_ge(loaded, 96)
            act.activation(gate[:, :, :], gate[:, :, :], ACT.Silu).then_inc(gate_done, 1)
            for n in range(LAT_UNITS):
                act.wait_ge(arg_done, n + 1)
                act.activation(sm[:, n % 2, :, :], sm[:, n % 2, :, :], ACT.Exp).then_inc(exp_done, 1)
            for t in range(TILES):
                act.wait_ge(gated, t + 1)
                act.activation(xs[:, t, :], Y[:, t, :], ACT.Square, accum_out=ss[:, t:t + 1]).then_inc(squared, 1)
            act.wait_ge(squared, TILES + 1)
            act.activation(std[:, :], ss[:, :], ACT.Sqrt).then_inc(std_done, 1)


GH, GE = 6, 64
GW = GH * GE
PAIRS = GH // 2
LEVELS = 7
ALLW = GH * P
REC = ALLW + 8
UNITS = 2 * T2


def gdn_prepare(nc, tag, tok, beta, cum, logs, q_n, k_n, v, qT, kT, inv_in, attn_out):
    with ExitStack() as ctx:
        sb = lambda n, s, d=F32: ctx.enter_context(nc.sbuf_tensor(f"{tag}_{n}", s, d))
        sem = own_semaphores(nc, ctx, tag)
        pbank = lambda n: ctx.enter_context(nc.psum_tensor(f"{tag}_{n}", [P, BANK], F32))
        ident, mask = sb("ident", [P, P]), sb("mask", [P, 2, P])
        sq = sb("sq", [P, 2, GW])
        norms, std = sb("norms", [P, T2, 2 * GH]), sb("std", [P, T2, 2 * GH])
        eps = sb("eps", [P, 1])
        kk = sb("kk", [P, 2, GH, P])
        kq = sb("kq", [P, 2, 2, GH, P])
        dec = sb("dec", [P, 2, GH, P])
        rec = sb("rec", [P, 2, REC])
        att = sb("att", [P, 2, GH, P])
        ps_r = [pbank("ps_r0"), pbank("ps_r1")]
        ps_kk = [pbank("ps_kk0"), pbank("ps_kk1")]
        ps_kq = [pbank("ps_kq0"), pbank("ps_kq1")]
        ps_t = [pbank("ps_t0"), pbank("ps_t1")]
        names = ("loaded", "consts", "squared", "summed", "std_done", "normed", "turned", "t_moved", "r_made", "g_made",
                 "arg_done", "kk_moved", "kq_masked", "exp_done", "rec_done", "att_done")
        (loaded, consts, squared, summed, std_done, normed, turned, t_moved, r_made, g_made,
         arg_done, kk_moved, kq_masked, exp_done, rec_done, att_done) = (sem(n) for n in names)
        rec_stored = [sem("rec_stored0"), sem("rec_stored1")]
        att_stored = [sem("att_stored0"), sem("att_stored1")]
        block = ctx.enter_context(nc.Block())
        slot = lambda t, d: next(2 * s + d for s in range(STEPS) if order(s, d) == t)

        @block.sync
        def _(sp):
            for n, dst in enumerate((q_n, k_n, v)):
                sp.dma_start(dst[:, :, :], tok[:, n * GW:(n + 1) * GW].rearrange("(t p) c -> p t c", p=P)).then_inc(loaded, 16)
            for t in range(T2):
                for d in range(2):
                    n = 2 * t + d
                    sp.wait_ge(rec_done, n + 1)
                    sp.dma_start(inv_in[slot(t, d)], rec[:, d, :]).then_inc(rec_stored[d], 16)
                    if t < TILES:
                        sp.wait_ge(att_done, n + 1)
                        sp.dma_start(attn_out[slot(t, d)], att[:, d, :, :].rearrange("p h i -> p (h i)")).then_inc(att_stored[d], 16)
            for d in range(2):
                sp.wait_ge(rec_stored[d], 16 * T2)
                sp.wait_ge(att_stored[d], 16 * TILES)

        @block.gpsimd
        def _(pool):
            make_identity(pool, ident)
            decay_masks(pool, mask)
            pool.memset(eps[:, :], EPS2)
            pool.memset(rec[:, :, ALLW:REC], 0.0)
            pool.drain()
            pool.memset(ident[0:1, 0:1], 1.0).then_inc(consts, 1)
            for t in range(T2):
                for d in range(2):
                    n = 2 * t + d
                    pool.wait_ge(exp_done, n + 1)
                    pool.wait_ge(kk_moved, 2 * t + 2)
                    wait(pool, rec_stored[d], 16 * t)
                    pool.tensor_copy(rec[:, d, ALLW:ALLW + GH], beta[:, t, d * GH:(d + 1) * GH])
                    pool.tensor_tensor(rec[:, d, 0:ALLW].rearrange("p (h i) -> p h i", h=GH), kk[:, t % 2, :, :], dec[:, d, :, :], ALU.mult)
                    pool.drain()
                    pool.memset(rec[0:1, d, REC - 1:REC], 0.0).then_inc(rec_done, 1)

        @block.tensor
        def _(pe):
            pe.wait_ge(consts, 1)

            def decays(n):
                t, d = n // 2, n % 2
                wait(pe, arg_done, n)
                for h in range(GH):
                    col = 2 * SH + d * GH + h
                    last = pe.matmul(ps_r[h // 3][:, (h % 3) * P:(h % 3 + 1) * P], logs[:, t, col:col + 1].to_broadcast([P, P]),
                                     mask[:, d, :], start=True, stop=True)
                last.then_inc(r_made, 1)

            for t in range(T2):
                cols = slice(t * P, (t + 1) * P)
                decays(2 * t)
                pe.wait_ge(normed, 2 * t + 2)
                for m, src in enumerate((q_n, k_n)):
                    wait(pe, t_moved, 2 * t + m - 1)
                    for g in range(PAIRS):
                        last = pe.transpose(ps_t[m][:, g * P:(g + 1) * P], src[:, t, g * P:(g + 1) * P], ident[:, :])
                    last.then_inc(turned, 1)
                wait(pe, kk_moved, 2 * t)
                wait(pe, kq_masked, 2 * t)
                pe.wait_ge(t_moved, 2 * t + 2)
                for h in range(GH):
                    rows = slice(GE * (h % 2), GE * (h % 2) + GE)
                    out = slice(h // 2 * P, (h // 2 + 1) * P)
                    pe.matmul(ps_kk[h % 2][:, out], kT[rows, h // 2, cols], kT[rows, h // 2, cols], start=True, stop=True)
                for h in range(GH):
                    rows = slice(GE * (h % 2), GE * (h % 2) + GE)
                    out = slice(h // 2 * P, (h // 2 + 1) * P)
                    last = pe.matmul(ps_kq[h % 2][:, out], kT[rows, h // 2, cols], qT[rows, h // 2, cols], start=True, stop=True)
                last.then_inc(g_made, 1)
                decays(2 * t + 1)

        @block.vector
        def _(dve):
            dve.wait_ge(loaded, 48)
            dve.wait_ge(consts, 1)
            for t in range(T2):
                for m, src in enumerate((q_n, k_n)):
                    dve.drain()
                    dve.tensor_tensor(sq[:, m, :], src[:, t, :], src[:, t, :], ALU.mult)
                    dve.drain()
                    dve.tensor_reduce(norms[:, t, m * GH:(m + 1) * GH], by_head(sq[:, m, :]), AX_X, ALU.add).then_inc(summed, 1)
            dve.wait_ge(std_done, 1)
            dve.reciprocal(norms[:, :, :], std[:, :, :])
            dve.drain()
            dve.tensor_scalar(norms[:, :, 0:GH], norms[:, :, 0:GH], GE ** -0.5, None, ALU.mult)
            dve.drain()

            def norm(t):
                for m, src in enumerate((q_n, k_n)):
                    dve.tensor_tensor(by_head(src[:, t, :]), by_head(src[:, t, :]), spread(norms[:, t, m * GH:(m + 1) * GH], GH, GE),
                                      ALU.mult).then_inc(normed, 1)

            def args(n):
                t, d = n // 2, n % 2
                dve.wait_ge(r_made, n + 1)
                wait(dve, rec_done, n - 1)
                wait(dve, att_done, min(n - 1, 2 * TILES))
                for h in range(GH):
                    col = 2 * SH + d * GH + h
                    last = dve.tensor_scalar(dec[:, d, h, :], ps_r[h // 3][:, (h % 3) * P:(h % 3 + 1) * P], cum[:, t, col:col + 1], 0.0,
                                             ALU.subtract, ALU.min)
                last.then_inc(arg_done, 1)

            def attend(n):
                t, d = n // 2, n % 2
                dve.wait_ge(exp_done, n + 1)
                wait(dve, att_stored[d], 16 * t)
                dve.tensor_tensor(att[:, d, :, :], kq[:, t % 2, d, :, :], dec[:, d, :, :], ALU.mult).then_inc(att_done, 1)

            norm(0)
            for t in range(T2):
                args(2 * t)
                if t + 1 < T2:
                    norm(t + 1)
                dve.wait_ge(g_made, t + 1)
                for m in range(2):
                    dve.drain()
                    for d in range(2):
                        out = kq[:, t % 2, d, :, :].rearrange("p (g m) i -> p m g i", m=2)[:, m]
                        last = dve.tensor_tensor(out, ps_kq[m][:, 0:PAIRS * P].rearrange("p (g i) -> p g i", g=PAIRS),
                                                 mask[:, d:d + 1, :].to_broadcast([P, PAIRS, P]), ALU.mult)
                    last.then_inc(kq_masked, 1)
                args(2 * t + 1)
                dve.drain()
                if t < TILES:
                    attend(2 * t)
                    attend(2 * t + 1)

        @block.scalar
        def _(act):
            act.wait_ge(summed, 2 * T2)
            act.wait_ge(consts, 1)
            act.activation(std[:, :, :], norms[:, :, :], ACT.Sqrt, bias=eps[:, 0:1]).then_inc(std_done, 1)
            for t in range(T2):
                for m, dst in enumerate((qT, kT)):
                    act.wait_ge(turned, 2 * t + m + 1)
                    act.activation(dst[:, :, t * P:(t + 1) * P], ps_t[m][:, 0:PAIRS * P].rearrange("p (g i) -> p g i", g=PAIRS),
                                   ACT.Copy).then_inc(t_moved, 1)
                act.wait_ge(arg_done, 2 * t + 1)
                act.activation(dec[:, 0, :, :], dec[:, 0, :, :], ACT.Exp).then_inc(exp_done, 1)
                act.wait_ge(g_made, t + 1)
                wait(act, rec_done, 2 * (t - 1))
                for m in range(2):
                    out = kk[:, t % 2, :, :].rearrange("p (g m) i -> p m g i", m=2)[:, m]
                    act.activation(out, ps_kk[m][:, 0:PAIRS * P].rearrange("p (g i) -> p g i", g=PAIRS), ACT.Copy).then_inc(kk_moved, 1)
                act.wait_ge(arg_done, 2 * t + 2)
                act.activation(dec[:, 1, :, :], dec[:, 1, :, :], ACT.Exp).then_inc(exp_done, 1)


def gdn_invert(nc, tag, inv_in, inv_out):
    with ExitStack() as ctx:
        sb = lambda n, s, d=F32: ctx.enter_context(nc.sbuf_tensor(f"{tag}_{n}", s, d))
        sem = own_semaphores(nc, ctx, tag)
        pbank = lambda n: ctx.enter_context(nc.psum_tensor(f"{tag}_{n}", [P, BANK], F32))
        ident, mask = sb("ident", [P, P]), sb("mask", [P, 2, LEVELS, P])
        hold = sb("hold", [1, 4])
        rec = sb("rec", [P, 2, 2, REC])
        nbeta = sb("nbeta", [P, 2, GH])
        T, TT = sb("T", [P, 2, GH, P]), sb("TT", [P, 2, GH, P])
        X = sb("X", [P, 2, GH, P])
        out = sb("out", [P, 2, GH, P])
        ps_x = [[pbank(f"ps_x{d}{g}") for g in range(2)] for d in range(2)]
        ps_y = [[pbank(f"ps_y{d}{g}") for g in range(2)] for d in range(2)]
        loaded = [[sem(f"loaded{d}{b}") for b in range(2)] for d in range(2)]
        stored = [sem("stored0"), sem("stored1")]
        consts, started = sem("consts"), [sem("started0"), sem("started1")]
        x_made, x_moved, y_made, y_taken, yt_made, yt_taken = ([sem(f"{n}{d}") for d in range(2)] for n in
                                                               ("x_made", "x_moved", "y_made", "y_taken", "yt_made", "yt_taken"))
        out_done = [sem("out_done0"), sem("out_done1")]
        block = ctx.enter_context(nc.Block())
        half = lambda t, g: t[:, 3 * g:3 * g + 3, :]
        bank = lambda b: b[:, 0:3 * P].rearrange("p (h i) -> p h i", h=3)

        def steps(eng, step):
            with eng.Fori(0, STEPS // 2) as i:
                step(i, 0)
                step(i, 1)

        @block.sync
        def _(sp):
            def load(i, b, unit):
                for d in range(2):
                    sp.dma_start(rec[:, d, b, :], inv_in[bass.ds(4 * i + 2 * unit + d, 1), :, :].rearrange("a p n -> p (a n)")).then_inc(loaded[d][b], 16)

            load(0, 0, 0)
            load(0, 1, 1)

            def store(s):
                for d in range(2):
                    sp.wait_ge(out_done[d], s + 1)
                    sp.dma_start(inv_out[bass.ds(2 * s + d, 1)].rearrange("a p n -> p (a n)"),
                                 out[:, d, :, :].rearrange("p h i -> p (h i)")).then_inc(stored[d], 16)

            with sp.Fori(0, STEPS // 2 - 1) as i:
                for b in range(2):
                    store(2 * i + b)
                    load(i, b, 2 + b)
            store(STEPS - 2)
            store(STEPS - 1)
            sp.wait_ge(stored[0], 16 * STEPS)
            sp.wait_ge(stored[1], 16 * STEPS)

        @block.gpsimd
        def _(pool):
            make_identity(pool, ident)
            pool.memset(mask[:, :, :, :], 0.0)
            pool.drain()
            for lev in range(LEVELS):
                b = 1 << lev
                G = P // (2 * b)
                for lower in (1, 0):
                    cols = mask[:, 1 - lower, lev, :].rearrange("p (g a c) -> p g a c", a=2, c=b)[:, :, 1 - lower, :]
                    pool.memset(cols, 1.0)
                    pool.drain()
                    pool.affine_select(out=cols, in_=cols, compare_op=ALU.is_ge, fill=0.0, base=-b * lower,
                                       pattern=[[-2 * b, G], [0, b]], channel_multiplier=1)
                    pool.drain()
                    pool.affine_select(out=cols, in_=cols, compare_op=ALU.is_ge, fill=0.0, base=b - 1 + b * lower,
                                       pattern=[[2 * b, G], [0, b]], channel_multiplier=-1)
                    pool.drain()
            pool.memset(ident[0:1, 0:1], 1.0).then_inc(consts, 1)

        @block.tensor
        def _(pe):
            pe.wait_ge(consts, 1)

            def step(i, b):
                n = 2 * i + b
                for lev in range(LEVELS):
                    at = LEVELS * n + lev
                    for d in range(2):
                        if lev == 0:
                            pe.wait_ge(started[d], n + 1)
                        pe.wait_ge(y_taken[d], (LEVELS - 1) * n + lev)
                        pe.wait_ge(yt_taken[d], at)
                        for h in range(GH):
                            last = pe.matmul(ps_x[d][h // 3][:, (h % 3) * P:(h % 3 + 1) * P], rec[:, d, b, h * P:(h + 1) * P],
                                             T[:, d, h, :], start=True, stop=True)
                        last.then_inc(x_made[d], 1)
                    for d in range(2):
                        pe.wait_ge(x_moved[d], at + 1)
                        if 0 < lev < LEVELS - 1:
                            for h in range(GH):
                                last = pe.matmul(ps_y[d][h // 3][:, (h % 3) * P:(h % 3 + 1) * P], TT[:, d, h, :], X[:, d, h, :], start=True, stop=True)
                            last.then_inc(y_made[d], 1)
                        for h in range(GH):
                            last = pe.matmul(ps_x[d][h // 3][:, (h % 3) * P:(h % 3 + 1) * P], X[:, d, h, :], TT[:, d, h, :], start=True, stop=True)
                        last.then_inc(yt_made[d], 1)
            steps(pe, step)

        @block.scalar
        def _(act):
            def step(i, b):
                n = 2 * i + b
                for lev in range(LEVELS):
                    at = LEVELS * n + lev
                    for d in range(2):
                        act.wait_ge(x_made[d], at + 1)
                        for h in range(GH):
                            last = act.activation(X[:, d, h, :], ps_x[d][h // 3][:, (h % 3) * P:(h % 3 + 1) * P], ACT.Copy, scale=nbeta[:, d, h:h + 1])
                        last.then_inc(x_moved[d], 1)
            steps(act, step)

        @block.vector
        def _(dve):
            dve.wait_ge(consts, 1)

            def step(i, b):
                n = 2 * i + b
                for d in range(2):
                    dve.wait_ge(loaded[d][b], 16 * i + 16)
                    dve.tensor_scalar(nbeta[:, d, :], rec[:, d, b, ALLW:ALLW + GH], -1.0, None, ALU.mult)
                    eye = ident[:, :].rearrange("p (a i) -> p a i", a=1).to_broadcast([P, GH, P])
                    dve.tensor_copy(T[:, d, :, :], eye)
                    dve.tensor_copy(TT[:, d, :, :], eye)
                    dve.drain()
                    dve.tensor_copy(nbeta[0:1, d, 0:1], nbeta[0:1, d, 0:1]).then_inc(started[d], 1)
                for lev in range(LEVELS):
                    at = LEVELS * n + lev
                    dve.drain()
                    for d in range(2):
                        if lev < LEVELS - 1:
                            if lev == 0:
                                dve.wait_ge(x_moved[d], at + 1)
                            else:
                                dve.wait_ge(y_made[d], (LEVELS - 2) * n + lev)
                            dve.memset(hold[:, 2 * d:2 * d + 1], 0.0)
                            for g in range(2):
                                m = mask[:, d, lev:lev + 1, :].to_broadcast([P, 3, P]).bitcast(U32)
                                last = dve.copy_predicated(half(T[:, d], g), m, bank(ps_y[d][g]) if lev else half(X[:, d], g))
                            last.then_inc(y_taken[d], 1)
                        dve.wait_ge(yt_made[d], at + 1)
                        dve.memset(hold[:, 2 * d + 1:2 * d + 2], 0.0)
                        for g in range(2):
                            m = mask[:, 1 - d, lev:lev + 1, :].to_broadcast([P, 3, P]).bitcast(U32)
                            last = dve.copy_predicated(half(TT[:, d], g), m, bank(ps_x[d][g]))
                        last.then_inc(yt_taken[d], 1)
                for d in range(2):
                    dve.drain()
                    dve.wait_ge(stored[d], 16 * n)
                    dve.tensor_copy(out[:, d, :, :], TT[:, d, :, :]).then_inc(out_done[d], 1)
                dve.drain()
            steps(dve, step)


def gdn_scan(nc, tag, inv, attn, q_n, k_n, v, qT, kT, beta, from_start, to_end, whole, gate_ab, norm_g, y_out):
    with ExitStack() as ctx:
        sb = lambda n, s, d=F32: ctx.enter_context(nc.sbuf_tensor(f"{tag}_{n}", s, d))
        sem = own_semaphores(nc, ctx, tag)
        pbank = lambda n: ctx.enter_context(nc.psum_tensor(f"{tag}_{n}", [P, BANK], F32))
        inv_t, att_t = sb("inv_t", [P, 4, ALLW]), sb("att_t", [P, 4, ALLW])
        square = sb("square", [P, P])
        zero = sb("zero", [P, GW])
        kw = sb("kw", [P, 2, GW])
        vb = sb("vb", [P, 2, GW])
        rate = sb("rate", [P, 2, T2, GH])
        col = sb("col", [P, 2, T2, PAIRS])
        rest, resid, new = sb("rest", [P, 2, GW]), sb("resid", [P, 2, GW]), sb("new", [P, 2, GW])
        inter, both = sb("inter", [P, 2, GW]), sb("both", [P, 2, GW])
        state, upd = sb("state", [P, 2, GW]), sb("upd", [P, GW])
        O, gate = sb("O", [P, TILES, GW]), sb("gate", [P, TILES, GW])
        norm, sq = sb("norm", [P, GE]), sb("sq", [P, TILES, GW])
        ss, std, eps = sb("ss", [P, TILES, GH]), sb("std", [P, TILES, GH]), sb("eps", [P, 1])
        ps_k, ps_q, ps_n, ps_o, ps_u = (pbank(f"ps_{n}") for n in "kqnou")
        names = ("vec_loaded", "consts", "kw_done", "vb_done", "k_made", "q_made", "resid_done", "new_made", "new_moved", "o_made",
                 "u_made", "state_done", "both_done", "o_added", "sq_done", "ss_done", "std_done", "gate_done", "y_done", "stored")
        (vec_loaded, consts, kw_done, vb_done, k_made, q_made, resid_done, new_made, new_moved, o_made,
         u_made, state_done, both_done, o_added, sq_done, ss_done, std_done, gate_done, y_done, stored) = (sem(n) for n in names)
        inv_loaded = [sem(f"inv_loaded{b}") for b in range(4)]
        att_loaded = [sem(f"att_loaded{b}") for b in range(4)]
        block = ctx.enter_context(nc.Block())
        FIRST = 2 * CTX_STEPS
        GC = 2 * SH

        def place(u):
            return order(u // 2, u % 2), u % 2

        @block.sync
        def _(sp):
            sp.dma_start(gate[:, :, :], gate_ab[0:SEQ, 0:GW].rearrange("(t p) c -> p t c", p=P)).then_inc(vec_loaded, 16)
            sp.dma_start(norm[:, :], row_to_all(norm_g, GE)).then_inc(vec_loaded, 16)
            for u in range(UNITS):
                wait(sp, new_made, u - 3)
                sp.dma_start(inv_t[:, u % 4, :], inv[u]).then_inc(inv_loaded[u % 4], 16)
                if u >= FIRST:
                    wait(sp, o_made, u - 3 - FIRST)
                    sp.dma_start(att_t[:, u % 4, :], attn[u]).then_inc(att_loaded[u % 4], 16)
            sp.wait_ge(y_done, TILES)
            for w in range(P // GRID_H):
                sp.dma_start(y_out.rearrange("(r t w) c -> w r t c", t=TILES, w=P // GRID_H)[w],
                             O[w * GRID_H:(w + 1) * GRID_H, :, :]).then_inc(stored, 16)
            sp.wait_ge(stored, 16 * P // GRID_H)

        @block.gpsimd
        def _(pool):
            pool.memset(eps[:, :], EPS2)
            pool.memset(square[:, :], 0.0)
            pool.memset(state[:, :, :], 0.0)
            pool.memset(O[:, :, :], 0.0)
            pool.drain()
            for h in range(2):
                part = slice(h * GE, (h + 1) * GE)
                pool.memset(square[part, part], 1.0)
                for d in range(2):
                    pool.tensor_copy(col[part, d, :, :],
                                     whole[part, :, GC + d * GH:GC + (d + 1) * GH].rearrange("p t (g h) -> p h t g", h=2)[:, h])
                    pool.drain()
            for d in range(2):
                pool.tensor_tensor(rate[:, d, :, :], beta[:, :, d * GH:(d + 1) * GH], from_start[:, :, GC + d * GH:GC + (d + 1) * GH], ALU.mult)
            pool.drain()
            pool.memset(eps[0:1, :], EPS2).then_inc(consts, 1)

            def ahead(u):
                t, d = place(u)
                wait(pool, u_made, u - 1)
                wait(pool, resid_done, u - 1)
                pool.tensor_tensor(by_head(vb[:, u % 2, :]), by_head(v[:, t, :]), spread(beta[:, t, d * GH:(d + 1) * GH], GH, GE), ALU.mult).then_inc(vb_done, 1)
                pool.tensor_tensor(by_head(kw[:, u % 2, :]), by_head(k_n[:, t, :]), spread(to_end[:, t, GC + d * GH:GC + (d + 1) * GH], GH, GE), ALU.mult).then_inc(kw_done, 1)

            def add(u):
                t, _ = place(u)
                pool.wait_ge(both_done, u - FIRST + 1)
                pool.tensor_tensor(O[:, t, :], O[:, t, :], both[:, u % 2, :], ALU.add).then_inc(o_added, 1)

            ahead(0)
            for u in range(UNITS):
                if u + 1 < UNITS:
                    ahead(u + 1)
                if u > FIRST:
                    pool.drain()
                    add(u - 1)
            pool.drain()
            add(UNITS - 1)

        @block.tensor
        def _(pe):
            pe.wait_ge(consts, 1)
            for u in range(UNITS):
                t, d = place(u)
                cols = slice(t * P, (t + 1) * P)
                wait(pe, state_done, u - 1)
                wait(pe, resid_done, u)
                for g in range(PAIRS):
                    last = pe.matmul(ps_k[:, g * P:(g + 1) * P], kT[:, g, cols], state[:, d, g * P:(g + 1) * P], start=True, stop=True)
                last.then_inc(k_made, 1)
                if u >= FIRST:
                    wait(pe, both_done, u - FIRST)
                    for g in range(PAIRS):
                        last = pe.matmul(ps_q[:, g * P:(g + 1) * P], qT[:, g, cols], state[:, d, g * P:(g + 1) * P], start=True, stop=True)
                    last.then_inc(q_made, 1)
                pe.wait_ge(resid_done, u + 1)
                pe.wait_ge(inv_loaded[u % 4], 16 * (u // 4 + 1))
                wait(pe, new_moved, u)
                for h in range(GH):
                    last = pe.matmul(ps_n[:, h * GE:(h + 1) * GE], inv_t[:, u % 4, h * P:(h + 1) * P], resid[:, u % 2, h * GE:(h + 1) * GE], start=True, stop=True)
                last.then_inc(new_made, 1)
                pe.wait_ge(new_moved, u + 1)
                if u < UNITS - 2:
                    pe.wait_ge(kw_done, u + 1)
                    wait(pe, state_done, u)
                    for g in range(PAIRS):
                        c = slice(g * P, (g + 1) * P)
                        last = pe.matmul(ps_u[:, c], kw[:, u % 2, c], new[:, u % 2, c], start=True, stop=True)
                    last.then_inc(u_made, 1)
                if u >= FIRST:
                    n = sum(1 for k in range(FIRST, u + 1) if k % 4 == u % 4)
                    pe.wait_ge(att_loaded[u % 4], 16 * n)
                    for h in range(GH):
                        last = pe.matmul(ps_o[:, h * GE:(h + 1) * GE], att_t[:, u % 4, h * P:(h + 1) * P], new[:, u % 2, h * GE:(h + 1) * GE], start=True, stop=True)
                    last.then_inc(o_made, 1)

        @block.vector
        def _(dve):
            dve.wait_ge(consts, 1)

            def out(u):
                t, d = place(u)
                dve.wait_ge(q_made, u - FIRST + 1)
                dve.tensor_tensor(by_head(inter[:, u % 2, :]), by_head(ps_q[:, 0:GW]), spread(from_start[:, t, GC + d * GH:GC + (d + 1) * GH], GH, GE), ALU.mult)
                dve.wait_ge(o_made, u - FIRST + 1)
                wait(dve, o_added, u - FIRST - 1)
                dve.drain()
                dve.tensor_tensor(both[:, u % 2, :], ps_o[:, 0:GW], inter[:, u % 2, :], ALU.add).then_inc(both_done, 1)

            for u in range(UNITS):
                t, d = place(u)
                dve.wait_ge(k_made, u + 1)
                dve.tensor_tensor(by_head(rest[:, u % 2, :]), by_head(ps_k[:, 0:GW]), spread(rate[:, d, t, :], GH, GE), ALU.mult)
                dve.wait_ge(vb_done, u + 1)
                wait(dve, new_made, u - 1)
                dve.drain()
                dve.tensor_tensor(resid[:, u % 2, :], vb[:, u % 2, :], rest[:, u % 2, :], ALU.subtract).then_inc(resid_done, 1)
                dve.wait_ge(new_made, u + 1)
                wait(dve, u_made, u - 1)
                wait(dve, o_made, u - 1 - FIRST)
                dve.tensor_copy(new[:, u % 2, :], ps_n[:, 0:GW]).then_inc(new_moved, 1)
                if u < UNITS - 2:
                    dve.wait_ge(u_made, u + 1)
                    dve.tensor_tensor(upd[:, :].rearrange("p (g c) -> p g c", g=PAIRS), ps_u[:, 0:GW].rearrange("p (g c) -> p g c", g=PAIRS),
                                      square[:, :].rearrange("p (a c) -> p a c", a=1).to_broadcast([P, PAIRS, P]), ALU.mult)
                    wait(dve, k_made, u + 1)
                    wait(dve, q_made, u - FIRST + 1)
                    dve.drain()
                    for g in range(PAIRS):
                        c = slice(g * P, (g + 1) * P)
                        last = dve.scalar_tensor_tensor(out=state[:, d, c], in0=state[:, d, c], scalar=col[:, d, t, g:g + 1], in1=upd[:, c],
                                                        op0=ALU.mult, op1=ALU.add)
                    last.then_inc(state_done, 1)
                    dve.drain()
                if u >= FIRST:
                    out(u)
            dve.wait_ge(o_added, UNITS - FIRST)
            for t in range(TILES):
                dve.tensor_tensor(sq[:, t, :], O[:, t, :], O[:, t, :], ALU.mult)
            dve.drain()
            dve.tensor_reduce(ss[:, :, :].rearrange("p t h -> p (t h)"), sq[:, :, :].rearrange("p t (h e) -> p (t h) e", e=GE), AX_X, ALU.add).then_inc(ss_done, 1)
            dve.wait_ge(std_done, 1)
            dve.reciprocal(ss[:, :, :], std[:, :, :])
            dve.drain()
            dve.wait_ge(gate_done, 1)
            for t in range(TILES):
                dve.tensor_tensor(by_head(O[:, t, :]), by_head(O[:, t, :]), spread(ss[:, t, :], GH, GE), ALU.mult)
                dve.tensor_tensor(by_head(gate[:, t, :]), by_head(gate[:, t, :]),
                                  norm[:, :].rearrange("p (a e) -> p a e", a=1).to_broadcast([P, GH, GE]), ALU.mult)
                dve.drain()
                dve.tensor_tensor(O[:, t, :], O[:, t, :], gate[:, t, :], ALU.mult).then_inc(y_done, 1)

        @block.scalar
        def _(act):
            act.wait_ge(vec_loaded, 32)
            act.activation(gate[:, :, :], gate[:, :, :], ACT.Silu).then_inc(gate_done, 1)
            act.wait_ge(ss_done, 1)
            act.activation(std[:, :, :], ss[:, :, :], ACT.Sqrt, scale=1.0 / GE, bias=eps[:, 0:1]).then_inc(std_done, 1)


def gdn(nc, tag, tok, gate_ab, norm_g, beta, cum, from_start, to_end, whole, logs, y_out):
    inv_in = nc.dram_tensor(f"{tag}_inv_in", [UNITS, P, REC], F32).ap()
    inv_out = nc.dram_tensor(f"{tag}_inv_out", [UNITS, P, ALLW], F32).ap()
    attn = nc.dram_tensor(f"{tag}_attn", [UNITS, P, ALLW], F32).ap()
    with ExitStack() as ctx:
        sb = lambda n, s: ctx.enter_context(nc.sbuf_tensor(f"{tag}_{n}", s, F32))
        q_n, k_n, v = (sb(n, [P, T2, GW]) for n in ("q_n", "k_n", "v"))
        qT, kT = (sb(n, [P, PAIRS, ROWS2]) for n in ("qT", "kT"))
        gdn_prepare(nc, f"{tag}p", tok, beta, cum, logs, q_n, k_n, v, qT, kT, inv_in, attn)
        gdn_invert(nc, f"{tag}i", inv_in, inv_out)
        gdn_scan(nc, f"{tag}s", inv_out, attn, q_n, k_n, v, qT, kT, beta, from_start, to_end, whole, gate_ab, norm_g, y_out)


EXPERTS = 16
FF = D // 2
CAP = 2 * SEQ // EXPERTS
NINF = -3.0e38


def close_mixer(nc, tag, x, x_next, pool_yT, y_ssd, y_gdn, w_out, ada, ada_bias, gate_at):
    POOLB = 2
    NY = KB - POOLB
    with ExitStack() as ctx:
        sb = lambda n, s, d=F32: ctx.enter_context(nc.sbuf_tensor(f"{tag}_{n}", s, d))
        sem = own_semaphores(nc, ctx, tag)
        pbank = lambda n: ctx.enter_context(nc.psum_tensor(f"{tag}_{n}", [P, BANK], F32))
        w = sb("w", [P, KB, D])
        vecs = sb("vecs", [P, 2, D])
        pT = sb("pT", [P, POOLB, SEQ])
        y = sb("y", [P, 2, 2, SW])
        xt = sb("xt", [P, 2, D])
        yT = sb("yT", [P, 2, NY, P])
        part = sb("part", [P, 2, D])
        ident = sb("ident", [P, P])
        ps_t = [[pbank(f"ps_t{a}{g}") for g in range(2)] for a in range(2)]
        ps_z = [[pbank(f"ps_z{a}{g}") for g in range(2)] for a in range(2)]
        w_loaded, vecs_loaded, consts = sem("w_loaded"), sem("vecs_loaded"), sem("consts")
        loaded = [sem("loaded0"), sem("loaded1")]
        stored = [sem("stored0"), sem("stored1")]
        turned, t_moved, made, scaled, done = (sem(n) for n in ("turned", "t_moved", "made", "scaled", "done"))
        block = ctx.enter_context(nc.Block())

        @block.sync
        def _(sp):
            def load(t):
                rows = slice(t * P, (t + 1) * P)
                wait(sp, done, t - 1)
                wait(sp, turned, 2 * (t - 1))
                for src, dst in ((y_ssd, y[:, t % 2, 0, :]), (y_gdn, y[:, t % 2, 1, :]), (x, xt[:, t % 2, :])):
                    sp.dma_start(dst, src[rows, :]).then_inc(loaded[t % 2], 16)

            load(0)
            sp.dma_start(pT[:, :, :], pool_yT.rearrange("(b p) t -> p b t", p=P)).then_inc(w_loaded, 16)
            sp.dma_start(w[:, :, :], w_out.rearrange("(k p) n -> p k n", p=P)).then_inc(w_loaded, 16)
            sp.dma_start(vecs[:, 0, :], row_to_all(ada[0, gate_at:gate_at + D], D)).then_inc(vecs_loaded, 16)
            sp.dma_start(vecs[:, 1, :], row_to_all(ada_bias[gate_at:gate_at + D], D)).then_inc(vecs_loaded, 16)
            for t in range(TILES):
                if t + 1 < TILES:
                    load(t + 1)
                sp.wait_ge(done, t + 1)
                sp.dma_start(x_next[t * P:(t + 1) * P, :], part[:, t % 2, :]).then_inc(stored[t % 2], 16)
            sp.wait_ge(stored[0], 8 * TILES)
            sp.wait_ge(stored[1], 8 * TILES)

        @block.gpsimd
        def _(pool):
            make_identity(pool, ident)
            pool.memset(ident[0:1, 0:1], 1.0).then_inc(consts, 1)
            for t in range(TILES):
                pool.wait_ge(scaled, t + 1)
                pool.tensor_tensor(part[:, t % 2, :], part[:, t % 2, :], xt[:, t % 2, :], ALU.add).then_inc(done, 1)

        @block.tensor
        def _(pe):
            pe.wait_ge(consts, 1)

            def turn(t):
                pe.wait_ge(loaded[t % 2], 48 * (t // 2 + 1))
                wait(pe, t_moved, 2 * (t - 1))
                for g in range(2):
                    for j in range(3):
                        last = pe.transpose(ps_t[t % 2][g][:, j * P:(j + 1) * P], y[:, t % 2, g, j * P:(j + 1) * P], ident[:, :])
                    last.then_inc(turned, 1)

            turn(0)
            pe.wait_ge(w_loaded, 32)
            for t in range(TILES):
                pe.wait_ge(t_moved, 2 * t + 2)
                wait(pe, scaled, t - 1)
                for h in range(2):
                    for k in range(KB):
                        lhsT = pT[:, k, t * P:(t + 1) * P] if k < POOLB else yT[:, t % 2, k - POOLB, :]
                        last = pe.matmul(ps_z[t % 2][h][:, :], lhsT, w[:, k, h * BANK:(h + 1) * BANK], start=(k == 0), stop=(k == KB - 1))
                last.then_inc(made, 1)
                if t + 1 < TILES:
                    turn(t + 1)

        @block.scalar
        def _(act):
            for t in range(TILES):
                wait(act, made, t - 1)
                for g in range(2):
                    act.wait_ge(turned, 2 * t + g + 1)
                    act.activation(yT[:, t % 2, 3 * g:3 * g + 3, :], ps_t[t % 2][g][:, 0:3 * P].rearrange("p (j c) -> p j c", j=3),
                                   ACT.Copy).then_inc(t_moved, 1)

        @block.vector
        def _(dve):
            dve.wait_ge(vecs_loaded, 32)
            dve.tensor_tensor(vecs[:, 0, :], vecs[:, 0, :], vecs[:, 1, :], ALU.add)
            dve.drain()
            for t in range(TILES):
                dve.wait_ge(made, t + 1)
                wait(dve, stored[t % 2], 16 * (t // 2))
                for h in range(2):
                    c = slice(h * BANK, (h + 1) * BANK)
                    last = dve.tensor_tensor(part[:, t % 2, c], ps_z[t % 2][h][:, :], vecs[:, 0, c], ALU.mult)
                last.then_inc(scaled, 1)


def route(nc, tag, hT, router_w, idx, gates):
    with ExitStack() as ctx:
        sb = lambda n, s, d=F32: ctx.enter_context(nc.sbuf_tensor(f"{tag}_{n}", s, d))
        sem = own_semaphores(nc, ctx, tag)
        pbank = lambda n: ctx.enter_context(nc.psum_tensor(f"{tag}_{n}", [P, BANK], F32))
        E = EXPERTS
        rw, ident = sb("rw", [P, KB, E]), sb("ident", [P, P])
        aff = sb("aff", [P, TILES, E])
        top, total = sb("top", [P, TILES]), sb("total", [P, TILES])
        affT = sb("affT", [E, SEQ])
        best, where, where_f = sb("best", [E, CAP]), sb("where", [E, CAP], U32), sb("where_f", [E, CAP])
        ps_l = pbank("ps_l")
        ps_a = [pbank("ps_a0"), pbank("ps_a1")]
        ps_i, ps_g = pbank("ps_i"), pbank("ps_g")
        loaded, consts, made, shifted, exp_done, aff_done, turned, picked, back = (
            sem(n) for n in ("loaded", "consts", "made", "shifted", "exp_done", "aff_done", "turned", "picked", "back"))
        block = ctx.enter_context(nc.Block())

        @block.sync
        def _(sp):
            sp.dma_start(rw[:, :, :], router_w.rearrange("(k p) e -> p k e", p=P)).then_inc(loaded, 16)

        @block.gpsimd
        def _(pool):
            make_identity(pool, ident)
            pool.memset(ident[0:1, 0:1], 1.0).then_inc(consts, 1)

        @block.tensor
        def _(pe):
            pe.wait_ge(consts, 1)
            pe.wait_ge(loaded, 16)
            for t in range(TILES):
                for k in range(KB):
                    last = pe.matmul(ps_l[:, t * E:(t + 1) * E], hT[:, k, t * P:(t + 1) * P], rw[:, k, :], start=(k == 0), stop=(k == KB - 1))
            last.then_inc(made, 1)
            pe.wait_ge(aff_done, 1)
            for t in range(TILES):
                last = pe.transpose(ps_a[t // 4][0:E, (t % 4) * P:(t % 4 + 1) * P], aff[:, t, :], ident[:, :])
            last.then_inc(turned, 1)
            pe.wait_ge(picked, 1)
            pe.transpose(ps_i[:, 0:E], where_f[:, :], ident[0:E, 0:E])
            pe.transpose(ps_g[:, 0:E], best[:, :], ident[0:E, 0:E]).then_inc(back, 1)

        @block.scalar
        def _(act):
            act.wait_ge(shifted, 1)
            act.activation(aff[:, :, :], aff[:, :, :], ACT.Exp).then_inc(exp_done, 1)

        @block.vector
        def _(dve):
            dve.wait_ge(made, 1)
            logits = ps_l[:, 0:TILES * E].rearrange("p (t e) -> p t e", e=E)
            along = lambda t: t[:, :].rearrange("p (t e) -> p t e", e=1).to_broadcast([P, TILES, E])
            dve.tensor_reduce(top[:, :], logits, AX_X, ALU.max)
            dve.drain()
            dve.tensor_tensor(aff[:, :, :], logits, along(top), ALU.subtract).then_inc(shifted, 1)
            dve.wait_ge(exp_done, 1)
            dve.tensor_reduce(total[:, :], aff[:, :, :], AX_X, ALU.add)
            dve.drain()
            dve.reciprocal(top[:, :], total[:, :])
            dve.drain()
            dve.tensor_tensor(aff[:, :, :], aff[:, :, :], along(top), ALU.mult).then_inc(aff_done, 1)
            dve.wait_ge(turned, 1)
            for g in range(2):
                dve.tensor_copy(affT[:, g * BANK:(g + 1) * BANK], ps_a[g][0:E, :])
            for r in range(CAP // 8):
                c = slice(8 * r, 8 * r + 8)
                dve.drain()
                dve.max(best[:, c], affT[:, :])
                dve.drain()
                dve.max_index(where[:, c], best[:, c], affT[:, :])
                dve.drain()
                dve.match_replace(affT[:, :], best[:, c], affT[:, :], NINF)
            dve.drain()
            dve.tensor_copy(where_f[:, :], where[:, :]).then_inc(picked, 1)
            dve.wait_ge(back, 1)
            dve.tensor_copy(idx[:, :], ps_i[:, 0:E])
            dve.tensor_copy(gates[:, :], ps_g[:, 0:E])


def load_expert(sp, weights, w_gate, w_up, w_down, e, b):
    wg, wu, wd, gu_loaded, d_loaded = weights
    for dst, w in ((wg, w_gate), (wu, w_up)):
        sp.dma_start(dst[:, b, :, :], w[bass.ds(e, 1)].rearrange("a (k p) f -> p (a k) f", p=P)).then_inc(gu_loaded[b], 16)
    sp.dma_start(wd[:, b, :, :], w_down[bass.ds(e, 1)].rearrange("a (k p) f -> p (a k) f", p=P)).then_inc(d_loaded[b], 16)


def start_experts(nc, ctx, tag, w_gate, w_up, w_down):
    sb = lambda n, s: ctx.enter_context(nc.sbuf_tensor(f"{tag}_{n}", s, F32))
    sem = own_semaphores(nc, ctx, tag)
    wg, wu, wd = sb("wg", [P, 2, KB, FF]), sb("wu", [P, 2, KB, FF]), sb("wd", [P, 2, FF // P, D])
    weights = (wg, wu, wd, [sem("gu_loaded0"), sem("gu_loaded1")], [sem("d_loaded0"), sem("d_loaded1")])
    with nc.Block() as block:
        @block.sync
        def _(sp):
            load_expert(sp, weights, w_gate, w_up, w_down, 0, 0)
            load_expert(sp, weights, w_gate, w_up, w_down, 1, 1)
    return weights


def experts(nc, tag, h, idx, gates, weights, w_gate, w_up, w_down, total):
    FB = FF // P
    with ExitStack() as ctx:
        sb = lambda n, s, d=F32: ctx.enter_context(nc.sbuf_tensor(f"{tag}_{n}", s, d))
        sem = own_semaphores(nc, ctx, tag)
        pbank = lambda n: ctx.enter_context(nc.psum_tensor(f"{tag}_{n}", [P, BANK], F32))
        ident = sb("ident", [P, P])
        hold = sb("hold", [1, 2])
        zero = sb("zero", [P, D])
        wg, wu, wd, gu_loaded, d_loaded = weights
        gate_now = sb("gate_now", [P, 2])
        idx_in = [sb(f"idx_in{b}", [P, 1], I32) for b in range(2)]
        idx_out = [sb(f"idx_out{b}", [P, 1], I32) for b in range(2)]
        xe = [sb("xe0", [P, D]), sb("xe1", [P, D])]
        ye = [sb("ye0", [P, D]), sb("ye1", [P, D])]
        xT = sb("xT", [P, 2, KB, P])
        act_g, hid, hidT = sb("act_g", [P, FF]), sb("hid", [P, FF]), sb("hidT", [P, FB, P])
        ps_t = [pbank("ps_t0"), pbank("ps_t1")]
        ps_g, ps_u, ps_h = pbank("ps_g"), pbank("ps_u"), pbank("ps_h")
        ps_d = [pbank("ps_d0"), pbank("ps_d1")]
        names = ("consts", "zeroed", "idx_set", "turned", "t_moved", "g_made", "u_made", "g_act", "hid_done", "h_turned", "h_moved",
                 "d_made", "y_done", "added")
        (consts, zeroed, idx_set, turned, t_moved, g_made, u_made, g_act, hid_done, h_turned, h_moved,
         d_made, y_done, added) = (sem(n) for n in names)
        gathered = [sem("gathered0"), sem("gathered1")]
        block = ctx.enter_context(nc.Block())

        @block.sync
        def _(sp):
            sp.wait_ge(consts, 1)
            for t in range(TILES):
                sp.dma_start(total[t * P:(t + 1) * P, :], zero[:, :]).then_inc(zeroed, 16)

            with sp.Fori(0, EXPERTS // 2 - 1) as i:
                for b in range(2):
                    sp.wait_ge(d_made, 2 * i + b + 1)
                    load_expert(sp, weights, w_gate, w_up, w_down, 2 * i + (b + 2), b)

        @block.gpsimd
        def _(pool):
            make_identity(pool, ident)
            pool.memset(hold[:, :], 0.0)
            pool.memset(zero[:, :], 0.0)
            pool.drain()
            pool.memset(ident[0:1, 0:1], 1.0).then_inc(consts, 1)
            pool.wait_ge(zeroed, 16 * TILES)

            def gather(i, b, e):
                pool.drain()
                pool.wait_ge(idx_set, e + 1)
                pool.tensor_tensor(hold[:, 0:1], zero[0:1, 0:1], zero[0:1, 0:1], ALU.add)
                pool.indirect_dma_start(out=xe[b][:, :], out_offset=None, in_=h,
                                        in_offset=bass.IndirectOffsetOnAxis(ap=idx_in[b][:, 0:1], axis=0)).then_inc(gathered[b], 16)

            def scatter(n, b):
                pool.drain()
                pool.wait_ge(y_done, n + 1)
                pool.tensor_tensor(hold[:, 0:1], zero[0:1, 0:1], zero[0:1, 0:1], ALU.add)
                pool.wait_ge(added, 16 * n)
                pool.tensor_tensor(hold[:, 1:2], zero[0:1, 0:1], zero[0:1, 0:1], ALU.add)
                pool.indirect_dma_start(out=total, out_offset=bass.IndirectOffsetOnAxis(ap=idx_out[b][:, 0:1], axis=0),
                                        in_=ye[b][:, :], in_offset=None, compute_op=ALU.add).then_inc(added, 16)

            gather(0, 0, 0)
            gather(0, 1, 1)
            with pool.Fori(0, EXPERTS // 2 - 1) as i:
                for b in range(2):
                    gather(i, b, 2 * i + (b + 2))
                    scatter(2 * i + b, b)
            scatter(EXPERTS - 2, 0)
            scatter(EXPERTS - 1, 1)
            pool.wait_ge(added, 16 * EXPERTS)

        @block.vector
        def _(dve):
            def choose(b, e):
                dve.tensor_copy(idx_in[b][:, :], idx[:, bass.ds(e, 1)]).then_inc(idx_set, 1)

            choose(0, 0)
            choose(1, 1)

            def one(i, b, more):
                n = 2 * i + b
                if more:
                    dve.wait_ge(gathered[b], 16 * i + 16)
                    dve.wait_ge(turned, 2 * n + 2)
                    choose(b, 2 * i + (b + 2))
                dve.tensor_copy(gate_now[:, b:b + 1], gates[:, bass.ds(n, 1)])
                dve.wait_ge(g_act, n + 1)
                dve.wait_ge(u_made, n + 1)
                dve.wait_ge(h_turned, n)
                dve.tensor_tensor(hid[:, :], act_g[:, :], ps_u[:, :], ALU.mult).then_inc(hid_done, 1)
                dve.wait_ge(d_made, n + 1)
                wait(dve, added, 32 * i + 16 * (b - 1))
                dve.tensor_copy(idx_out[b][:, :], idx[:, bass.ds(n, 1)])
                dve.tensor_scalar(ye[b][:, 0:BANK], ps_d[0][:, :], gate_now[:, b:b + 1], None, ALU.mult)
                dve.tensor_scalar(ye[b][:, BANK:D], ps_d[1][:, :], gate_now[:, b:b + 1], None, ALU.mult).then_inc(y_done, 1)

            one(0, 0, True)
            one(0, 1, True)
            with dve.Fori(1, EXPERTS // 2 - 1) as i:
                one(i, 0, True)
                one(i, 1, True)
            one(EXPERTS // 2 - 1, 0, False)
            one(EXPERTS // 2 - 1, 1, False)

        @block.scalar
        def _(act):
            def move_x(n, b):
                for g in range(2):
                    act.wait_ge(turned, 2 * n + g + 1)
                    act.activation(xT[:, b, 4 * g:4 * g + 4, :], ps_t[g][:, :].rearrange("p (j c) -> p j c", j=4), ACT.Copy).then_inc(t_moved, 1)

            def one(i, b, more):
                n = 2 * i + b
                act.wait_ge(g_made, n + 1)
                act.wait_ge(hid_done, n)
                act.activation(act_g[:, :], ps_g[:, :], ACT.Silu).then_inc(g_act, 1)
                if more:
                    move_x(n + 1, 1 - b)
                act.wait_ge(h_turned, n + 1)
                act.wait_ge(d_made, n)
                act.activation(hidT[:, :, :], ps_h[:, :].rearrange("p (j c) -> p j c", j=FB), ACT.Copy).then_inc(h_moved, 1)

            move_x(0, 0)
            with act.Fori(0, EXPERTS // 2 - 1) as i:
                one(i, 0, True)
                one(i, 1, True)
            one(EXPERTS // 2 - 1, 0, True)
            one(EXPERTS // 2 - 1, 1, False)

        @block.tensor
        def _(pe):
            pe.wait_ge(consts, 1)

            def turn(i, b, n):
                pe.wait_ge(gathered[b], 16 * i + 16)
                pe.wait_ge(t_moved, 2 * n)
                for g in range(2):
                    for j in range(4):
                        k = 4 * g + j
                        last = pe.transpose(ps_t[g][:, j * P:(j + 1) * P], xe[b][:, k * P:(k + 1) * P], ident[:, :])
                    last.then_inc(turned, 1)

            def one(i, b, more):
                n = 2 * i + b
                pe.wait_ge(gu_loaded[b], 32 * i + 32)
                pe.wait_ge(t_moved, 2 * n + 2)
                pe.wait_ge(g_act, n)
                for k in range(KB):
                    last = pe.matmul(ps_g[:, :], xT[:, b, k, :], wg[:, b, k, :], start=(k == 0), stop=(k == KB - 1))
                last.then_inc(g_made, 1)
                pe.wait_ge(hid_done, n)
                for k in range(KB):
                    last = pe.matmul(ps_u[:, :], xT[:, b, k, :], wu[:, b, k, :], start=(k == 0), stop=(k == KB - 1))
                last.then_inc(u_made, 1)
                if more:
                    turn(i if b == 0 else i + 1, 1 - b, n + 1)
                pe.wait_ge(hid_done, n + 1)
                pe.wait_ge(h_moved, n)
                for j in range(FB):
                    last = pe.transpose(ps_h[:, j * P:(j + 1) * P], hid[:, j * P:(j + 1) * P], ident[:, :])
                last.then_inc(h_turned, 1)
                pe.wait_ge(h_moved, n + 1)
                pe.wait_ge(d_loaded[b], 16 * i + 16)
                pe.wait_ge(y_done, n)
                for g in range(2):
                    for j in range(FB):
                        last = pe.matmul(ps_d[g][:, :], hidT[:, j, :], wd[:, b, j, g * BANK:(g + 1) * BANK], start=(j == 0), stop=(j == FB - 1))
                last.then_inc(d_made, 1)

            turn(0, 0, 0)
            with pe.Fori(0, EXPERTS // 2 - 1) as i:
                one(i, 0, True)
                one(i, 1, True)
            one(EXPERTS // 2 - 1, 0, True)
            one(EXPERTS // 2 - 1, 1, False)


def finish(nc, tag, x, total, ada, ada_bias, gate_at, gain, out):
    with ExitStack() as ctx:
        sb = lambda n, s, d=F32: ctx.enter_context(nc.sbuf_tensor(f"{tag}_{n}", s, d))
        sem = own_semaphores(nc, ctx, tag)
        vecs = sb("vecs", [P, 3, D])
        NB = 4
        xt, tt, o = sb("xt", [P, NB, D]), sb("tt", [P, NB, D]), sb("o", [P, NB, D])
        sq = sb("sq", [P, D])
        ss, std, rstd, eps = (sb(n, [P, NB]) for n in ("ss", "std", "rstd", "eps"))
        vec_loaded, consts, scaled, summed, std_done, done = (sem(n) for n in ("vec_loaded", "consts", "scaled", "summed", "std_done", "done"))
        loaded = [sem(f"loaded{b}") for b in range(NB)]
        stored = [sem(f"stored{b}") for b in range(NB)]
        block = ctx.enter_context(nc.Block())

        @block.sync
        def _(sp):
            for n, src in enumerate((ada[0, gate_at:gate_at + D], ada_bias[gate_at:gate_at + D], gain)):
                sp.dma_start(vecs[:, n, :], row_to_all(src, D)).then_inc(vec_loaded, 16)

            def load(t):
                wait(sp, done, t - NB + 1)
                sp.dma_start(tt[:, t % NB, :], total[t * P:(t + 1) * P, :]).then_inc(loaded[t % NB], 16)
                sp.dma_start(xt[:, t % NB, :], x[t * P:(t + 1) * P, :]).then_inc(loaded[t % NB], 16)

            for t in range(NB - 1):
                load(t)
            for t in range(TILES):
                if t + NB - 1 < TILES:
                    load(t + NB - 1)
                sp.wait_ge(done, t + 1)
                sp.dma_start(out[t * P:(t + 1) * P, :], o[:, t % NB, :]).then_inc(stored[t % NB], 16)
            for b in range(NB):
                sp.wait_ge(stored[b], 16 * TILES // NB)

        @block.gpsimd
        def _(pool):
            pool.memset(eps[:, :], EPS2).then_inc(consts, 1)
            for t in range(TILES):
                b = t % NB
                pool.wait_ge(scaled, t + 1)
                pool.tensor_tensor(tt[:, b, :], tt[:, b, :], xt[:, b, :], ALU.add).then_inc(summed, 1)

        @block.scalar
        def _(act):
            act.wait_ge(consts, 1)
            for t in range(TILES):
                b = t % NB
                act.wait_ge(summed, t + 1)
                act.activation(sq[:, :], tt[:, b, :], ACT.Square, accum_out=ss[:, b:b + 1])
                act.drain()
                act.activation(std[:, b:b + 1], ss[:, b:b + 1], ACT.Sqrt, scale=1.0 / D, bias=eps[:, 0:1]).then_inc(std_done, 1)

        @block.vector
        def _(dve):
            dve.wait_ge(vec_loaded, 48)
            dve.tensor_tensor(vecs[:, 0, :], vecs[:, 0, :], vecs[:, 1, :], ALU.add)
            dve.drain()

            def scale(t):
                dve.wait_ge(loaded[t % NB], 32 * (t // NB + 1))
                dve.tensor_tensor(tt[:, t % NB, :], tt[:, t % NB, :], vecs[:, 0, :], ALU.mult).then_inc(scaled, 1)

            scale(0)
            scale(1)
            for t in range(TILES):
                b = t % NB
                if t + 2 < TILES:
                    scale(t + 2)
                dve.wait_ge(std_done, t + 1)
                dve.reciprocal(rstd[:, b:b + 1], std[:, b:b + 1])
                wait(dve, stored[b], 16 * (t // NB))
                dve.drain()
                dve.scalar_tensor_tensor(out=o[:, b, :], in0=tt[:, b, :], scalar=rstd[:, b:b + 1], in1=vecs[:, 2, :],
                                         op0=ALU.mult, op1=ALU.mult).then_inc(done, 1)


Z_WIDTH = 384
SSD_WIDTH = 896
DT_WIDTH = 12
QKV_WIDTH = 1152
GATE_AB = 408


def network(nc, x, w_in_ab, gla_gate_up, gla_gate_bias, gla_norm, w_out_ab, w_in_c, hgrn_bounds, hgrn_norm, w_out_c,
            rel_bias, ln_gain, ln_bias, c_2, ctx_2, c_ctx_2, norm1_g_2, norm2_g_2, ada_w_2, ada_b_2, w_in_2, w_out_2,
            pool_w_2, pool_scale_2, ssd_conv_w_2, ssd_conv_b_2, ssd_a_log_2, ssd_dt_bias_2, ssd_d_2, ssd_norm_g_2,
            gdn_conv_w_2, gdn_a_log_2, gdn_dt_bias_2, gdn_norm_g_2, router_w_2, exp_w_gate_2, exp_w_up_2,
            exp_w_down_2, final_norm_g_2, buckets, out):
    dram = lambda name, *shape: nc.dram_tensor(name, list(shape), F32).ap()
    A, B, C = 512, 1024, 1536
    x1, x2, x3, h = (dram(n, SEQ, D) for n in ("x1", "x2", "x3", "h"))
    ada = dram("ada", 2, 6 * D)
    alpha = 2 ** 0.5
    scale = P ** -0.5

    with nc.sbuf_tensor("xT", [P, KB, SEQ], F32) as xT:
        transpose_in(nc, "tin", x[0], xT, SEQ)

        vpad, vectors, attn = dram("vpad", SEQ + 2 * VPAD, A), dram("vectors", AH, 3 * VEC), dram("attn", 3, SEQ, A + 16)
        qa, ka, qb, kb = (dram(n, A, SEQ) for n in ("qa", "ka", "qb", "kb"))
        vb, low, gate_l0 = dram("vb", SEQ, B), dram("low", 2 * RANK, SEQ), dram("gate_l0", SEQ, A + B)
        gla_g = [dram(f"gla_g{d}", A, SEQ) for d in range(2)]
        gla_o = [dram(f"gla_o{d}", SEQ, B) for d in range(2)]
        bias_vectors(nc, "bv", rel_bias, buckets, vectors, vpad)
        with nc.sbuf_tensor("sT", [P, KB, 2], F32) as sT:
            condition(nc, "cond", c_2, c_ctx_2, sT)
            w = w_in_ab[0]
            project(nc, "in0", [
                Job(CHANNEL, xT, SEQ, w, 0, 256, 2, qa),
                Job(CHANNEL, xT, SEQ, w, A, 256, 2, ka),
                Job(TOKEN, xT, SEQ, w, 2 * A, 256, 2, vpad[VPAD:VPAD + SEQ, :]),
                Job(CHANNEL, xT, SEQ, w, 3 * A, 256, 2, qb),
                Job(CHANNEL, xT, SEQ, w, 4 * A, 256, 2, kb),
                Job(TOKEN, xT, SEQ, w, 5 * A, 256, 4, vb),
                Job(CHANNEL, xT, SEQ, w, 5 * A + B, 2 * RANK, 1, low),
                Job(TOKEN, xT, SEQ, w, 5 * A + B + 2 * RANK, 256, 6, gate_l0),
                Job(TOKEN, sT, 2, ada_w_2[0], 0, 256, 24, ada),
            ])
        low_rank_gates(nc, "low", low, gla_gate_up[0], gla_gate_bias[0], gla_g)
        dilated_attention(nc, "att", qa, ka, vpad, vectors, attn)
        gated_scan(nc, "gla", 4, B // 4, qb, vb, gla_o, kT=kb, gT=gla_g, g_scale=1 / 16, q_scale=scale)
        close_layer(nc, "end0", x[0], x1, xT, gla_o, gate_l0, gla_norm[0], w_out_ab[0], ln_gain[0], ln_bias[0],
                    B // 4, alpha, attn=attn, attn_heads=AH)

        hq, hf0, hf1 = (dram(n, C, SEQ) for n in ("hq", "hf0", "hf1"))
        hv, gate_l1 = dram("hv", SEQ, C), dram("gate_l1", SEQ, C)
        hgrn_o = [dram(f"hgrn_o{d}", SEQ, C) for d in range(2)]
        w = w_in_c[0]
        project(nc, "in1", [
            Job(CHANNEL, xT, SEQ, w, 0, 256, 6, hq),
            Job(CHANNEL, xT, SEQ, w, C, 256, 6, hf0),
            Job(CHANNEL, xT, SEQ, w, 2 * C, 256, 6, hf1),
            Job(TOKEN, xT, SEQ, w, 3 * C, 256, 6, hv),
            Job(TOKEN, xT, SEQ, w, 4 * C, 256, 6, gate_l1),
        ])
        gated_scan(nc, "hgrn", C // P, P, hq, hv, hgrn_o, zT=[hf0, hf1], bounds=hgrn_bounds, q_scale=scale)
        close_layer(nc, "end1", x1, x2, xT, hgrn_o, gate_l1, hgrn_norm[0], w_out_c[0], ln_gain[1], ln_bias[1], P, alpha)

    poolT, pooledT = dram("poolT", 2 * P, SEQ), dram("pooledT", 2 * P, SEQ)
    z, dt_raw = dram("z", SEQ, Z_WIDTH), dram("dt_raw", ROWS2, DT_WIDTH)
    xbcT, xbc = dram("xbcT", SSD_WIDTH, ROWS2), dram("xbc", ROWS2, SSD_WIDTH)
    bcT = dram("bcT", SSD_WIDTH - Z_WIDTH, ROWS2)
    qkvT, qkv, gate_ab = dram("qkvT", QKV_WIDTH, ROWS2), dram("qkv", ROWS2, QKV_WIDTH), dram("gate_ab", ROWS2, GATE_AB)
    y_ssd, y_gdn = dram("y_ssd", SEQ, Z_WIDTH), dram("y_gdn", SEQ, Z_WIDTH)
    with ExitStack() as ctx:
        sb = lambda n, s: ctx.enter_context(nc.sbuf_tensor(n, s, F32))
        hT, hT_cols, hcT = sb("hT", [P, KB, SEQ]), sb("hT_cols", [P, KB, SEQ]), sb("hcT", [P, KB, CTX])
        modulate(nc, "mod1", x2, SEQ, norm1_g_2[0], ada, ada_b_2[0], 0, 0, D, hT, hT_cols)
        modulate(nc, "modc", ctx_2[0], CTX, norm1_g_2[0], ada, ada_b_2[0], 1, 0, D, hcT)
        w = w_in_2[0]
        xbc_at = 2 * P + Z_WIDTH
        dt_at = xbc_at + SSD_WIDTH
        qkv_at = dt_at + DT_WIDTH
        gate_at = qkv_at + QKV_WIDTH
        ab_at = gate_at + Z_WIDTH
        lat, con = slice(0, SEQ), slice(SEQ, ROWS2)
        project(nc, "in2", [
            Job(CHANNEL, hT, SEQ, w, 0, 256, 1, poolT),
            Job(TOKEN, hT, SEQ, w, 2 * P, 192, 2, z),
            Job(CHANNEL, hT, SEQ, w, xbc_at, 256, 3, xbcT[:, lat]),
            Job(CHANNEL, hT, SEQ, w, xbc_at + 768, 128, 1, xbcT[768:SSD_WIDTH, lat]),
            Job(TOKEN, hT, SEQ, w, dt_at, DT_WIDTH, 1, dt_raw[lat, :]),
            Job(CHANNEL, hT_cols, SEQ, w, qkv_at, 256, 4, qkvT[:, lat]),
            Job(CHANNEL, hT_cols, SEQ, w, qkv_at + 1024, 128, 1, qkvT[1024:QKV_WIDTH, lat]),
            Job(TOKEN, hT_cols, SEQ, w, gate_at, GATE_AB // 2, 2, gate_ab[lat, :]),
            Job(CHANNEL, hcT, CTX, w, xbc_at, 256, 3, xbcT[:, con]),
            Job(CHANNEL, hcT, CTX, w, xbc_at + 768, 128, 1, xbcT[768:SSD_WIDTH, con]),
            Job(TOKEN, hcT, CTX, w, dt_at, DT_WIDTH, 1, dt_raw[con, :]),
            Job(CHANNEL, hcT, CTX, w, qkv_at, 256, 4, qkvT[:, con]),
            Job(CHANNEL, hcT, CTX, w, qkv_at + 1024, 128, 1, qkvT[1024:QKV_WIDTH, con]),
            Job(TOKEN, hcT, CTX, w, ab_at, 2 * DT_WIDTH, 1, gate_ab[con, Z_WIDTH:GATE_AB]),
        ])
    pool_branch(nc, "pool", poolT, pool_w_2[0], pool_scale_2[0], pooledT)
    conv_silu(nc, "cssd", xbcT, ssd_conv_w_2[0], ssd_conv_b_2[0], xbc, bcT, Z_WIDTH)
    conv_silu(nc, "cgdn", qkvT, gdn_conv_w_2[0], None, qkv)
    with ExitStack() as ctx:
        table = lambda n, w: ctx.enter_context(nc.sbuf_tensor(n, [P, T2, w], F32))
        dt, beta = table("dt", 12), table("beta", 12)
        decays = [table(n, 24) for n in ("cum", "from_start", "to_end", "whole", "logs")]
        token_decays(nc, "dec", dt_raw, ssd_dt_bias_2[0], ssd_a_log_2[0], gate_ab, gdn_dt_bias_2[0], gdn_a_log_2[0],
                     dt, beta, *decays)
        ssd_scan(nc, "ssd", xbc, bcT, z, ssd_d_2[0], ssd_norm_g_2[0], dt, *decays, y_ssd)
        gdn(nc, "gdn", qkv, gate_ab, gdn_norm_g_2[0], beta, *decays, y_gdn)
    close_mixer(nc, "mix", x2, x3, pooledT, y_ssd, y_gdn, w_out_2[0], ada, ada_b_2[0], 2 * D)

    total = dram("total", SEQ, D)
    with ExitStack() as ctx:
        weights = start_experts(nc, ctx, "expw", exp_w_gate_2[0], exp_w_up_2[0], exp_w_down_2[0])
        idx = ctx.enter_context(nc.sbuf_tensor("idx", [P, EXPERTS], I32))
        gates = ctx.enter_context(nc.sbuf_tensor("gates", [P, EXPERTS], F32))
        with nc.sbuf_tensor("hT2", [P, KB, SEQ], F32) as hT:
            modulate(nc, "mod2", x3, SEQ, norm2_g_2[0], ada, ada_b_2[0], 0, 3 * D, 4 * D, hT, None, h)
            route(nc, "route", hT, router_w_2[0], idx, gates)
        experts(nc, "exp", h, idx, gates, weights, exp_w_gate_2[0], exp_w_up_2[0], exp_w_down_2[0], total)
    finish(nc, "fin", x3, total, ada, ada_b_2[0], 5 * D, final_norm_g_2, out[0])


_INS = ['x', 'w_in_ab', 'gla_gate_up', 'gla_gate_bias', 'gla_norm', 'w_out_ab', 'w_in_c', 'hgrn_lower_bounds',
        'hgrn_norm', 'w_out_c', 'rel_bias', 'ln_gain', 'ln_bias', 'c_2', 'ctx_2', 'c_ctx_2', 'norm1_g_2', 'norm2_g_2',
        'ada_w_2', 'ada_b_2', 'w_in_2', 'w_out_2', 'pool_w_2', 'pool_scale_2', 'ssd_conv_w_2', 'ssd_conv_b_2',
        'ssd_a_log_2', 'ssd_dt_bias_2', 'ssd_d_2', 'ssd_norm_g_2', 'gdn_conv_w_2', 'gdn_a_log_2', 'gdn_dt_bias_2',
        'gdn_norm_g_2', 'router_w_2', 'exp_w_gate_2', 'exp_w_up_2', 'exp_w_down_2', 'final_norm_g_2']


def kernel(**inputs):
    import numpy as _np
    import concourse.bacc as _bacc
    from concourse import mybir as _mybir
    from concourse.bass_utils import run_bass_kernel_spmd as _run

    nc = _bacc.Bacc("TRN2", target_bir_lowering=False, num_devices=1)
    arrays, args = {}, []
    for name in _INS:
        a = _np.asarray(inputs[name])
        if name == "hgrn_lower_bounds":
            a = a.T
        arrays[f"in_{name}_dram"] = _np.ascontiguousarray(a)
    arrays["in_buckets_dram"] = _np.ascontiguousarray(bucket_constant().reshape(REL_BUCKETS + 1, -1))
    for name, a in arrays.items():
        args.append(nc.dram_tensor(name, a.shape, _mybir.dt.from_np(a.dtype), kind="ExternalInput").ap())
    args.append(nc.dram_tensor("out_0_dram", (1, SEQ, D), F32, kind="ExternalOutput").ap())
    network(nc, *args)
    r = _run(nc, [arrays], core_ids=[0])
    return r.results[0]["out_0_dram"]
```
